# Optimizing a Trainium2 kernel written in Bass

```python
import math
import jax
import jax.numpy as jnp
from jax import lax
import numpy as np

D_MODEL = 1024
BATCH = 1
SEQ = 512
DEPTH = 2
DEC_BATCH = 8
DEC_SEQ = 8
PAST_LEN = 512
PAGE_SIZE = 128

N_MIXERS = 2
N_FOX_LAYERS = (DEPTH + 1) // 2
N_MLSTM_LAYERS = DEPTH // 2

FOX_HEADS = 16
FOX_HEAD_DIM = D_MODEL // FOX_HEADS
FOX_Q_BLOCK = 128
FOX_IN = 3 * D_MODEL + FOX_HEADS

MLSTM_HEADS = 8
MLSTM_DV = D_MODEL // MLSTM_HEADS
MLSTM_DK = MLSTM_DV // 2
MLSTM_CHUNK = 64
MLSTM_IN = 2 * MLSTM_HEADS * MLSTM_DK + 2 * D_MODEL + 2 * MLSTM_HEADS

MOE_GROUPS = 4
MOE_EXPERTS_PER_GROUP = 8
MOE_EXPERTS = MOE_GROUPS * MOE_EXPERTS_PER_GROUP
MOE_TOP_K = 2
MOE_HIDDEN = 256

RMS_EPS = 1e-6
F32 = jnp.float32

kernel_name = 'hybrid_fox_mlstm_hmoe_step'

def rmsnorm(x, g):
    xf = x.astype(F32)
    y = xf * lax.rsqrt(jnp.mean(xf * xf, axis=-1, keepdims=True) + RMS_EPS)
    return (y * g.astype(F32)).astype(x.dtype)

def gather_pages(pool, page_table):
    pages = pool[page_table]
    return pages.reshape(page_table.shape[0], page_table.shape[1] * pool.shape[1], *pool.shape[2:])

def fox_project(h, w_in, b_f):
    bsz, t, _ = h.shape
    proj = h @ w_in
    q = proj[..., :D_MODEL].reshape(bsz, t, FOX_HEADS, FOX_HEAD_DIM)
    k = proj[..., D_MODEL:2 * D_MODEL].reshape(bsz, t, FOX_HEADS, FOX_HEAD_DIM)
    v = proj[..., 2 * D_MODEL:3 * D_MODEL].reshape(bsz, t, FOX_HEADS, FOX_HEAD_DIM)
    log_f = jax.nn.log_sigmoid(proj[..., 3 * D_MODEL:].astype(F32) + b_f.astype(F32))
    return q, k, v, log_f

def fox_attention(q, k, v, c_q, c_k, q_offset):
    bsz, t_q, n_h, d_h = q.shape
    blk = math.gcd(t_q, FOX_Q_BLOCK)
    n_blk = t_q // blk
    k_pos = jnp.arange(k.shape[1])
    kf = k.astype(F32)
    vf = v.astype(F32)
    ck_h = c_k.astype(F32).transpose(0, 2, 1)
    scale = d_h ** -0.5

    def one_block(bi):
        start = bi * blk
        qb = lax.dynamic_slice_in_dim(q, start, blk, axis=1).astype(F32)
        cb = lax.dynamic_slice_in_dim(c_q, start, blk, axis=1).astype(F32).transpose(0, 2, 1)
        q_pos = q_offset + start + jnp.arange(blk)
        s = jnp.einsum('bqhd,bkhd->bhqk', qb, kf) * scale + (cb[..., :, None] - ck_h[..., None, :])
        s = jnp.where(k_pos[None, :] <= q_pos[:, None], s, -jnp.inf)
        p = jax.nn.softmax(s, axis=-1)
        return jnp.einsum('bhqk,bkhd->bqhd', p, vf)

    out = lax.map(one_block, jnp.arange(n_blk))
    return out.transpose(1, 0, 2, 3, 4).reshape(bsz, t_q, n_h, d_h).astype(q.dtype)

def fox_output(o, w_out):
    bsz, t = o.shape[:2]
    return o.reshape(bsz, t, D_MODEL) @ w_out

def mlstm_chunkwise(q, k, v, i_pre, log_f, c0, n0, m0):
    bsz, t = q.shape[:2]
    chunk = math.gcd(t, MLSTM_CHUNK)
    n_chunks = t // chunk

    def to_chunks(a):
        return a.reshape(bsz, n_chunks, chunk, *a.shape[2:]).swapaxes(0, 1)

    qs = to_chunks(q.astype(F32) * (MLSTM_DK ** -0.5))
    ks = to_chunks(k.astype(F32))
    vs = to_chunks(v.astype(F32))
    i_s = to_chunks(i_pre.astype(F32))
    f_s = to_chunks(log_f.astype(F32))
    causal = jnp.tril(jnp.ones((chunk, chunk), dtype=bool))

    def step(carry, inp):
        c_prev, n_prev, m_prev = carry
        qc, kc, vc, ic, fc = inp
        b = jnp.cumsum(fc, axis=1).transpose(0, 2, 1)
        ih = ic.transpose(0, 2, 1)
        d_mat = jnp.where(causal, b[..., :, None] - b[..., None, :] + ih[..., None, :], -jnp.inf)
        inter = b + m_prev[..., None]
        m_t = jnp.maximum(inter, jnp.max(d_mat, axis=-1))
        w_inter = jnp.exp(inter - m_t)
        s = jnp.exp(d_mat - m_t[..., None]) * jnp.einsum('blhd,bshd->bhls', qc, kc)
        num = jnp.einsum('bhls,bshv->bhlv', s, vc) + w_inter[..., None] * jnp.einsum('blhd,bhdv->bhlv', qc, c_prev)
        den = jnp.sum(s, axis=-1) + w_inter * jnp.einsum('blhd,bhd->bhl', qc, n_prev)
        h = num / jnp.maximum(jnp.abs(den), jnp.exp(-m_t))[..., None]
        b_last = b[..., -1]
        decay = b_last[..., None] - b + ih
        m_new = jnp.maximum(b_last + m_prev, jnp.max(decay, axis=-1))
        w_k = jnp.exp(decay - m_new[..., None])
        carry_scale = jnp.exp(b_last + m_prev - m_new)
        c_new = carry_scale[..., None, None] * c_prev + jnp.einsum('bhs,bshd,bshv->bhdv', w_k, kc, vc)
        n_new = carry_scale[..., None] * n_prev + jnp.einsum('bhs,bshd->bhd', w_k, kc)
        return (c_new, n_new, m_new), h.transpose(0, 2, 1, 3)

    (c_f, n_f, m_f), hs = lax.scan(step, (c0.astype(F32), n0.astype(F32), m0.astype(F32)),
                                   (qs, ks, vs, i_s, f_s))
    h = hs.swapaxes(0, 1).reshape(bsz, t, MLSTM_HEADS, MLSTM_DV)
    return h, c_f, n_f, m_f

def mlstm_mixer(h, w_in, b_i, b_f, head_norm, w_out, c0, n0, m0):
    bsz, t, _ = h.shape
    proj = h @ w_in
    qk = MLSTM_HEADS * MLSTM_DK
    q = proj[..., :qk].reshape(bsz, t, MLSTM_HEADS, MLSTM_DK)
    k = proj[..., qk:2 * qk].reshape(bsz, t, MLSTM_HEADS, MLSTM_DK)
    v = proj[..., 2 * qk:2 * qk + D_MODEL].reshape(bsz, t, MLSTM_HEADS, MLSTM_DV)
    o = proj[..., 2 * qk + D_MODEL:2 * qk + 2 * D_MODEL]
    gates = proj[..., 2 * qk + 2 * D_MODEL:].astype(F32)
    i_pre = gates[..., :MLSTM_HEADS] + b_i.astype(F32)
    log_f = jax.nn.log_sigmoid(gates[..., MLSTM_HEADS:] + b_f.astype(F32))
    hh, c_f, n_f, m_f = mlstm_chunkwise(q, k, v, i_pre, log_f, c0, n0, m0)
    hh = hh * lax.rsqrt(jnp.mean(hh * hh, axis=-1, keepdims=True) + RMS_EPS) * head_norm.astype(F32)
    out = (jax.nn.sigmoid(o.astype(F32)) * hh.reshape(bsz, t, D_MODEL)).astype(h.dtype) @ w_out
    return out, c_f, n_f, m_f

def hier_moe(h, w_group, b_group, w_router, b_router, w_gate, w_up, w_down):
    bsz, t, _ = h.shape
    x = h.reshape(bsz * t, D_MODEL)
    n_tok = x.shape[0]
    g_logits = (x @ w_group).astype(F32) + b_group.astype(F32)
    g_sel = jnp.argmax(g_logits, axis=-1)
    p_g = jnp.max(jax.nn.softmax(g_logits, axis=-1), axis=-1)
    e_logits = ((x @ w_router).astype(F32) + b_router.astype(F32)).reshape(n_tok, MOE_GROUPS, MOE_EXPERTS_PER_GROUP)
    e_in = e_logits[jnp.arange(n_tok), g_sel]
    top_v, top_i = lax.top_k(e_in, MOE_TOP_K)
    top_w = jax.nn.softmax(top_v, axis=-1) * p_g[:, None]
    expert_id = g_sel[:, None] * MOE_EXPERTS_PER_GROUP + top_i
    gates = jnp.sum(jax.nn.one_hot(expert_id, MOE_EXPERTS, dtype=F32) * top_w[..., None], axis=1)
    hg = jnp.einsum('nd,edf->nef', x, w_gate)
    hu = jnp.einsum('nd,edf->nef', x, w_up)
    act = jax.nn.silu(hg) * hu * gates[:, :, None].astype(hg.dtype)
    y = jnp.einsum('nef,efd->nd', act, w_down)
    return y.reshape(bsz, t, D_MODEL)

def setup_inputs(seed: int = 0) -> dict:
    key = jax.random.key(seed)
    ks = jax.random.split(key, 32)
    n_pages = PAST_LEN // PAGE_SIZE
    n_used = DEC_BATCH * n_pages
    n_pool = n_used + max(1, n_used // 4)
    d_in_scale = D_MODEL ** -0.5

    def nrm(k, shape, scale=1.0):
        return jax.random.normal(k, shape, F32) * scale

    x_prompt = nrm(ks[0], (BATCH, SEQ, D_MODEL))
    x_sample = nrm(ks[1], (DEC_BATCH, DEC_SEQ, D_MODEL))
    cache_k = nrm(ks[2], (N_FOX_LAYERS, n_pool, PAGE_SIZE, FOX_HEADS, FOX_HEAD_DIM))
    cache_v = nrm(ks[3], (N_FOX_LAYERS, n_pool, PAGE_SIZE, FOX_HEADS, FOX_HEAD_DIM))
    cache_logf = jax.nn.log_sigmoid(
        jax.random.uniform(ks[4], (N_FOX_LAYERS, n_pool, PAGE_SIZE, FOX_HEADS), F32, 1.0, 5.0)
        + nrm(ks[5], (N_FOX_LAYERS, n_pool, PAGE_SIZE, FOX_HEADS), 0.5))
    page_table = jax.random.permutation(ks[6], n_pool)[:n_used].reshape(DEC_BATCH, n_pages).astype(jnp.int32)
    state_C = nrm(ks[7], (N_MLSTM_LAYERS, DEC_BATCH, MLSTM_HEADS, MLSTM_DK, MLSTM_DV), 0.5)
    state_n = nrm(ks[8], (N_MLSTM_LAYERS, DEC_BATCH, MLSTM_HEADS, MLSTM_DK), 0.5)
    state_m = nrm(ks[9], (N_MLSTM_LAYERS, DEC_BATCH, MLSTM_HEADS))

    norm_mix = 1.0 + nrm(ks[10], (DEPTH, D_MODEL), 0.05)
    norm_ffn = 1.0 + nrm(ks[11], (DEPTH, D_MODEL), 0.05)
    norm_final = 1.0 + nrm(ks[12], (D_MODEL,), 0.05)

    fox_w_in = nrm(ks[13], (N_FOX_LAYERS, D_MODEL, FOX_IN), d_in_scale)
    fox_b_f = jax.random.uniform(ks[14], (N_FOX_LAYERS, FOX_HEADS), F32, 1.0, 5.0)
    fox_w_out = nrm(ks[15], (N_FOX_LAYERS, D_MODEL, D_MODEL), d_in_scale)

    mlstm_w_in = nrm(ks[16], (N_MLSTM_LAYERS, D_MODEL, MLSTM_IN), d_in_scale)
    mlstm_b_i = nrm(ks[17], (N_MLSTM_LAYERS, MLSTM_HEADS), 0.1)
    mlstm_b_f = jax.random.uniform(ks[18], (N_MLSTM_LAYERS, MLSTM_HEADS), F32, 3.0, 6.0)
    mlstm_head_norm = 1.0 + nrm(ks[19], (N_MLSTM_LAYERS, MLSTM_HEADS, MLSTM_DV), 0.05)
    mlstm_w_out = nrm(ks[20], (N_MLSTM_LAYERS, D_MODEL, D_MODEL), d_in_scale)

    moe_w_group = nrm(ks[21], (DEPTH, D_MODEL, MOE_GROUPS), d_in_scale)
    moe_b_group = nrm(ks[22], (DEPTH, MOE_GROUPS), 0.01)
    moe_w_router = nrm(ks[23], (DEPTH, D_MODEL, MOE_EXPERTS), d_in_scale)
    moe_b_router = nrm(ks[24], (DEPTH, MOE_EXPERTS), 0.01)
    moe_w_gate = nrm(ks[25], (DEPTH, MOE_EXPERTS, D_MODEL, MOE_HIDDEN), d_in_scale)
    moe_w_up = nrm(ks[26], (DEPTH, MOE_EXPERTS, D_MODEL, MOE_HIDDEN), d_in_scale)
    moe_w_down = nrm(ks[27], (DEPTH, MOE_EXPERTS, MOE_HIDDEN, D_MODEL), MOE_HIDDEN ** -0.5)

    return {
        'x_prompt': x_prompt, 'x_sample': x_sample,
        'cache_k': cache_k, 'cache_v': cache_v, 'cache_logf': cache_logf, 'page_table': page_table,
        'state_C': state_C, 'state_n': state_n, 'state_m': state_m,
        'norm_mix': norm_mix, 'norm_ffn': norm_ffn, 'norm_final': norm_final,
        'fox_w_in': fox_w_in, 'fox_b_f': fox_b_f, 'fox_w_out': fox_w_out,
        'mlstm_w_in': mlstm_w_in, 'mlstm_b_i': mlstm_b_i, 'mlstm_b_f': mlstm_b_f,
        'mlstm_head_norm': mlstm_head_norm, 'mlstm_w_out': mlstm_w_out,
        'moe_w_group': moe_w_group, 'moe_b_group': moe_b_group,
        'moe_w_router': moe_w_router, 'moe_b_router': moe_b_router,
        'moe_w_gate': moe_w_gate, 'moe_w_up': moe_w_up, 'moe_w_down': moe_w_down,
    }

def reference(x_prompt, x_sample, cache_k, cache_v, cache_logf, page_table, state_C, state_n, state_m,
              norm_mix, norm_ffn, norm_final, fox_w_in, fox_b_f, fox_w_out,
              mlstm_w_in, mlstm_b_i, mlstm_b_f, mlstm_head_norm, mlstm_w_out,
              moe_w_group, moe_b_group, moe_w_router, moe_b_router, moe_w_gate, moe_w_up, moe_w_down):
    xp, xs = x_prompt, x_sample
    k_p, v_p, lf_p, k_s, v_s, lf_s = [], [], [], [], [], []
    c_p, n_p, m_p, c_s, n_s, m_s = [], [], [], [], [], []
    for layer in range(DEPTH):
        hp = rmsnorm(xp, norm_mix[layer])
        hs = rmsnorm(xs, norm_mix[layer])
        j = layer // N_MIXERS
        if layer % N_MIXERS == 0:
            qp, kp, vp, lfp = fox_project(hp, fox_w_in[j], fox_b_f[j])
            cp = jnp.cumsum(lfp, axis=1)
            op = fox_attention(qp, kp, vp, cp, cp, 0)
            qs, kss, vss, lfs = fox_project(hs, fox_w_in[j], fox_b_f[j])
            k_past = gather_pages(cache_k[j], page_table)
            v_past = gather_pages(cache_v[j], page_table)
            lf_past = gather_pages(cache_logf[j], page_table)
            past_len = k_past.shape[1]
            k_all = jnp.concatenate([k_past.astype(kss.dtype), kss], axis=1)
            v_all = jnp.concatenate([v_past.astype(vss.dtype), vss], axis=1)
            c_all = jnp.cumsum(jnp.concatenate([lf_past.astype(F32), lfs], axis=1), axis=1)
            os_ = fox_attention(qs, k_all, v_all, c_all[:, past_len:], c_all, past_len)
            xp = xp + fox_output(op, fox_w_out[j])
            xs = xs + fox_output(os_, fox_w_out[j])
            k_p.append(kp); v_p.append(vp); lf_p.append(lfp)
            k_s.append(kss); v_s.append(vss); lf_s.append(lfs)
        else:
            bp = xp.shape[0]
            zc = jnp.zeros((bp, MLSTM_HEADS, MLSTM_DK, MLSTM_DV), F32)
            zn = jnp.zeros((bp, MLSTM_HEADS, MLSTM_DK), F32)
            zm = jnp.zeros((bp, MLSTM_HEADS), F32)
            op, cpf, npf, mpf = mlstm_mixer(hp, mlstm_w_in[j], mlstm_b_i[j], mlstm_b_f[j],
                                            mlstm_head_norm[j], mlstm_w_out[j], zc, zn, zm)
            os_, csf, nsf, msf = mlstm_mixer(hs, mlstm_w_in[j], mlstm_b_i[j], mlstm_b_f[j],
                                             mlstm_head_norm[j], mlstm_w_out[j],
                                             state_C[j], state_n[j], state_m[j])
            xp = xp + op
            xs = xs + os_
            c_p.append(cpf); n_p.append(npf); m_p.append(mpf)
            c_s.append(csf); n_s.append(nsf); m_s.append(msf)
        xp = xp + hier_moe(rmsnorm(xp, norm_ffn[layer]), moe_w_group[layer], moe_b_group[layer],
                           moe_w_router[layer], moe_b_router[layer],
                           moe_w_gate[layer], moe_w_up[layer], moe_w_down[layer])
        xs = xs + hier_moe(rmsnorm(xs, norm_ffn[layer]), moe_w_group[layer], moe_b_group[layer],
                           moe_w_router[layer], moe_b_router[layer],
                           moe_w_gate[layer], moe_w_up[layer], moe_w_down[layer])
    y_prompt = rmsnorm(xp, norm_final)
    y_sample = rmsnorm(xs, norm_final)
    return (y_prompt, y_sample,
            jnp.stack(k_p), jnp.stack(v_p), jnp.stack(lf_p),
            jnp.stack(k_s), jnp.stack(v_s), jnp.stack(lf_s),
            jnp.stack(c_p), jnp.stack(n_p), jnp.stack(m_p),
            jnp.stack(c_s), jnp.stack(n_s), jnp.stack(m_s))


_drawn_inputs = setup_inputs


def setup_inputs(seed=0):
    import zlib

    import numpy as np

    out = dict(_drawn_inputs(seed))
    spreads = {}
    factors = {}
    for name, (base, spread) in spreads.items():
        noise = np.random.default_rng([zlib.crc32(name.encode()), seed]).standard_normal(out[name].shape)
        drawn = base * np.exp(spread * noise) if base else spread * noise
        out[name] = jnp.asarray(drawn.astype(out[name].dtype))
    for name, factor in factors.items():
        out[name] = (out[name] * factor).astype(out[name].dtype)
    return out
```

```python
from contextlib import ExitStack

import numpy as np

import concourse.bass as bass
from concourse import mybir

F32 = mybir.dt.float32
I32 = mybir.dt.int32
U32 = mybir.dt.uint32
ALU = mybir.AluOpType
ACT = mybir.ActivationFunctionType
AX = mybir.AxisListType.X

P = 128
D = 1024
KC = D // P
PROMPT, SB, SS = 512, 8, 8
SAMP = SB * SS
NT = PROMPT // P + 1
TOK = PROMPT + SAMP
ROWS = [P] * (NT - 1) + [SAMP]
FH, FD = 16, 64
PAIRS = FH // 2
PAGE, NPAGE = 128, 4
PAST = PAGE * NPAGE
MH, MK, MV = 8, 64, 128
MPAIRS = MH // 2
GROUPS, PER, EXP, HID = 4, 8, 32, 256
LG = GROUPS + EXP
SLOT = 64
RING = 3
TILES = -(-((2 * TOK - EXP) // SLOT + EXP) // RING) * RING
SET = 40
FULL = 2 * TOK // SLOT
EPS = 1e-6
NEG = -1e30

CONSTS = [("ident", P), ("neg_causal", P), ("neg_causal_t", P), ("before", P), ("ones", PAST + SS),
          ("head_rows", P), ("dec_mask", SB * SAMP), ("samp_mask_t", SAMP), ("same", SB),
          ("selpair", MPAIRS * P), ("iota_slot", SLOT), ("iota_tile", TILES),
          ("rev4", GROUPS), ("rev32", EXP), ("token", NT), ("valid", NT), ("minus_half", MH * NT)]
OFFSET, CW = {}, 0
for _name, _w in CONSTS:
    OFFSET[_name] = (CW, _w)
    CW += _w


def constants():
    c = {n: np.zeros((P, w), np.float32) for n, w in CONSTS}
    i, r = np.arange(P)[:, None], np.arange(P)[None, :]
    c["ident"][:] = i == r
    c["neg_causal"][:] = np.where(r <= i, 0, NEG)
    c["neg_causal_t"][:] = np.where(i <= r, 0, NEG)
    c["before"][:] = i < r
    c["ones"][:] = 1
    c["head_rows"][:] = (i == r // SS) & (i < FH)
    b, k = np.arange(SB)[None, :, None], np.arange(SAMP)[None, None, :]
    q = (np.arange(P) % SS)[:, None, None]
    c["dec_mask"][:] = np.where((k // SS == b) & (k % SS <= q), 0, NEG).reshape(P, -1)
    s, t = i, np.arange(SAMP)[None, :]
    c["samp_mask_t"][:] = np.where((s // SS == t // SS) & (s <= t), 0, NEG)
    c["same"][:] = i // SS == np.arange(SB)[None, :]
    hp, p2 = np.arange(MPAIRS)[None, :, None], np.arange(P)[None, None, :]
    c["selpair"][:] = (i[:, :, None] == 2 * hp + p2 // MK).reshape(P, -1)
    c["iota_slot"][:] = np.arange(SLOT)
    c["iota_tile"][:] = np.arange(TILES)
    c["rev4"][:] = GROUPS - np.arange(GROUPS)
    c["rev32"][:] = EXP - np.arange(EXP)
    tok = np.arange(NT)[None, :] * P + i
    c["valid"][:] = tok < TOK
    c["token"][:] = np.where(tok < TOK, tok, 0)
    c["minus_half"][:] = -0.5
    return np.concatenate([c[n] for n, _ in CONSTS], 1)


class Chain:

    def __init__(self, eng, sem, base=0):
        self.eng, self.sem, self.base, self.n = eng, sem, base, 0

    def step(self, ins):
        self.n += 1
        return ins.then_inc(self.sem, 1)

    def wait(self):
        self.eng.wait_ge(self.sem, self.base + self.n)

    def __call__(self, ins):
        self.step(ins)
        self.wait()


def trunk(nc, i, o):
    with ExitStack() as ctx:
        def lasting(name):
            return ctx.enter_context(nc.semaphore(name))

        phases = []
        sets = [[lasting(f"set{n}_{k}") for k in range(SET)] for n in range(2)]
        taken = []

        def sem(name):
            while len(taken) <= len(phases):
                taken.append([])
            taken[len(phases)].append(name)
            return sets[len(phases) % 2][len(taken[len(phases)]) - 1]

        def sb(name, shape, dt=F32, where=ctx):
            return where.enter_context(nc.sbuf_tensor(name, shape, dt))

        ps = ctx.enter_context(nc.psum_tensor("ps", [P, 8, 512], F32))
        psf = ps[:].rearrange("p b n -> p (b n)")
        ps2 = ps[:].rearrange("p (c b) n -> p c (b n)", b=2)

        h_dram = [nc.dram_tensor(f"h_rows{n}", (TOK, D), F32, kind="Internal").ap() for n in range(2)]
        y_dram = nc.dram_tensor("expert_rows", (TILES * SLOT, D), F32, kind="Internal").ap()
        negc_dram = nc.dram_tensor("negc_rows", (FH, PROMPT), F32, kind="Internal").ap()

        cst = sb("cst", [P, CW])
        x = sb("x", [P, NT, D])
        rows = sb("rows", [P, NT, D])
        turned = sb("turned", [P, KC, TOK])
        gains = sb("gains", [P, 4, KC])
        sq = sb("sq", [P, NT])
        ms = sb("ms", [P, NT])
        rstd = sb("rstd", [P, NT])

        def const(name, p=P):
            at, w = OFFSET[name]
            return cst[0:p, at:at + w]

        ident = const("ident")

        passed = lasting("passed")

        def alone(eng):
            eng.sem_inc(passed, 1)


        const_in, x_in, gains_in = lasting("const_in"), lasting("x_in"), lasting("gains_in")
        zeroed = lasting("zeroed")

        def start_sp(sp):
            sp.dma_start(cst[:], i["consts"]).then_inc(const_in, 16)
            sp.dma_start(x[:, 0:NT - 1, :], i["x_prompt"].rearrange("a (n p) d -> p (a n) d", p=P)).then_inc(x_in, 16)
            sp.dma_start(x[0:SAMP, NT - 1, :], i["x_sample"].rearrange("b s d -> (b s) d")).then_inc(x_in, 16)
            for layer in range(2):
                for k, g in ((0, i["norm_mix"]), (1, i["norm_ffn"])):
                    sp.dma_start(gains[:, 2 * layer + k, :],
                                 g[layer, :].rearrange("(p c) -> p c", c=KC)).then_inc(gains_in, 16)
            sp.wait_ge(gains_in, 64)
            sp.wait_ge(const_in, 16)
            sp.wait_ge(x_in, 32)

        def start_dve(dve):
            dve.memset(sq[:], 1.0).then_inc(zeroed, 1)
            dve.wait_ge(zeroed, 1)

        phases.append(dict(sp=start_sp, dve=start_dve))

        def norm(tag, gain, keep=None):
            squared, meaned, rooted = sem(tag + "_squared"), sem(tag + "_meaned"), sem(tag + "_rooted")
            scaled, flipped = sem(tag + "_scaled"), sem(tag + "_flipped")
            gained_a, gained_v = sem(tag + "_gained_a"), sem(tag + "_gained_v")
            kept = sem(tag + "_kept")

            def act_(act):
                for n, r in enumerate(ROWS):
                    act.activation(rows[0:r, n, :], x[0:r, n, :], ACT.Square,
                                   accum_out=sq[0:r, n:n + 1]).then_inc(squared, 1)
                if gain is not None:
                    for c in range(0, KC, 2):
                        act.wait_ge(flipped, c + 1)
                        act.activation(turned[:, c, :], ps2[:, c % 4, 0:TOK], ACT.Copy,
                                       scale=gain[:, c:c + 1]).then_inc(gained_a, 1)

            def dve_(dve):
                dve.wait_ge(squared, NT)
                dve.tensor_scalar(ms[:], sq[:], 1.0 / D, EPS, ALU.mult, ALU.add).then_inc(meaned, 1)
                dve.wait_ge(rooted, 1)
                for n, r in enumerate(ROWS):
                    dve.tensor_scalar(rows[0:r, n, :], x[0:r, n, :], rstd[0:r, n:n + 1], None,
                                      ALU.mult).then_inc(scaled, 1)
                if gain is not None:
                    for c in range(1, KC, 2):
                        dve.wait_ge(flipped, c + 1)
                        dve.tensor_scalar(turned[:, c, :], ps2[:, c % 4, 0:TOK], gain[:, c:c + 1], None,
                                          ALU.mult).then_inc(gained_v, 1)

            def pool_(pool):
                pool.wait_ge(meaned, 1)
                pool.tensor_tensor(rstd[:], ms[:], const("minus_half")[:, 0:NT], ALU.pow).then_inc(rooted, 1)

            def pe_(pe):
                for c in range(KC):
                    if c >= 4:
                        pe.wait_ge((gained_a, gained_v)[c % 2], (c - 4) // 2 + 1)
                    for n, r in enumerate(ROWS):
                        if c == 0:
                            pe.wait_ge(scaled, n + 1)
                        mm = pe.transpose(ps2[:, c % 4, n * P:n * P + r], rows[0:r, n, c:D:KC], ident[0:r, 0:r])
                    mm.then_inc(flipped, 1)

            def sp_(sp):
                sp.wait_ge(scaled, NT)
                sp.dma_start(keep[0:PROMPT, :].rearrange("(n p) d -> p n d", p=P),
                             rows[:, 0:NT - 1, :]).then_inc(kept, 16)
                sp.dma_start(keep[PROMPT:TOK, :], rows[0:SAMP, NT - 1, :]).then_inc(kept, 16)
                sp.wait_ge(kept, 32)

            out = dict(act=act_, dve=dve_, pool=pool_)
            if gain is not None:
                out["pe"] = pe_
            if keep is not None:
                out["sp"] = sp_
            phases.append(out)

        def project_out(tag, w_dram, tiles, where):
            w = sb(tag + "_w", [P, KC, D], where=where)
            w_in, flipped, copied = sem(tag + "_w_in"), sem(tag + "_flipped"), sem(tag + "_copied")
            multiplied, added = sem(tag + "_multiplied"), sem(tag + "_added")

            def sp_(sp):
                sp.dma_start(w[:], w_dram.rearrange("(c p) n -> p c n", p=P)).then_inc(w_in, 16)

            def pe_(pe):
                for n in range(tiles):
                    r = ROWS[n]
                    if n >= 2:
                        pe.wait_ge(copied, n - 1)
                    for c in range(KC):
                        mm = pe.transpose(psf[:, (n % 2) * 1024 + c * P:(n % 2) * 1024 + c * P + r],
                                          rows[0:r, n, c * P:(c + 1) * P], ident[0:r, 0:r])
                    mm.then_inc(flipped, 1)
                pe.wait_ge(w_in, 16)
                for n in range(NT):
                    r = ROWS[n]
                    pe.wait_ge(copied, min(n + 1, tiles))
                    if n >= 2:
                        pe.wait_ge(added, n - 1)
                    for half in range(2):
                        for c in range(KC):
                            mm = pe.matmul(ps[0:r, 4 + 2 * (n % 2) + half, :], turned[:, c, n * P:n * P + r],
                                           w[:, c, half * 512:half * 512 + 512], start=(c == 0), stop=(c == KC - 1))
                    mm.then_inc(multiplied, 1)

            def act_(act):
                for n in range(tiles):
                    act.wait_ge(flipped, n + 1)
                    act.activation(turned[:, :, n * P:n * P + ROWS[n]],
                                   psf[:, (n % 2) * 1024:(n % 2) * 1024 + 1024].rearrange("p (c t) -> p c t", t=P)[:, :, 0:ROWS[n]],
                                   ACT.Copy).then_inc(copied, 1)

            def dve_(dve):
                for n in range(NT):
                    dve.wait_ge(multiplied, n + 1)
                    dve.tensor_tensor(x[0:ROWS[n], n, :], x[0:ROWS[n], n, :],
                                      ps2[0:ROWS[n], 2 + n % 2, :], ALU.add).then_inc(added, 1)

            phases.append(dict(sp=sp_, pe=pe_, act=act_, dve=dve_))

        def log_sigmoid_act(act, neg_abs, e, u, lnu, bent, rounded, logged):
            act.wait_ge(bent, 1)
            act.activation(e, neg_abs, ACT.Exp).then_inc(rounded, 1)
            act.wait_ge(bent, 2)
            act.activation(lnu, u, ACT.Ln).then_inc(logged, 1)

        def log_sigmoid_dve(dve, ch, out, z, neg_abs, e, u, lnu, bent, rounded, logged):
            ch(dve.scalar_tensor_tensor(neg_abs, z, -1.0, z, ALU.mult, ALU.min))
            dve.sem_inc(bent, 1)
            dve.wait_ge(rounded, 1)
            ch(dve.tensor_scalar(u, e, 1.0, None, ALU.add))
            dve.sem_inc(bent, 1)
            ch(dve.scalar_tensor_tensor(e, u, -1.0, e, ALU.add, ALU.subtract))
            dve.wait_ge(logged, 1)
            ch(dve.reciprocal(neg_abs, u))
            ch(dve.tensor_tensor(e, e, neg_abs, ALU.mult))
            ch(dve.tensor_tensor(lnu, lnu, e, ALU.subtract))
            ch(dve.scalar_tensor_tensor(out, z, 0.0, lnu, ALU.min, ALU.subtract))

        def fox():
            norm("fox_norm", gains[:, 0, :])
            fx = ExitStack()
            qT = sb("qT", [P, PAIRS, TOK], where=fx)
            kT = sb("kT", [P, PAIRS, TOK], where=fx)
            v = sb("v", [P, NT, D], where=fx)
            negc = sb("negc", [P, SB, PAST + SS], where=fx)
            pages = sb("pages", [1, SB * NPAGE], I32, where=fx)
            small = ExitStack()
            wblk = sb("wblk", [P, 3, KC, 512], where=small)
            wf = sb("wf", [P, KC, FH], where=small)
            bf = sb("bf", [FH, 1], where=small)
            z, neg_abs, e, u, lnu = (wblk[0:FH, 0].rearrange("p c n -> p (c n)")[:, n * TOK:(n + 1) * TOK]
                                     for n in range(5))
            lf = sb("flf", [FH, TOK], where=small)
            negp = sb("negp", [FH, PROMPT], where=small)
            lfs = wblk[0:FH, 1:3].rearrange("p r c n -> p (r c n)")[:, 0:SB * (PAST + SS)].rearrange(
                "p (b t) -> p b t", b=SB)
            lf_nat = sb("lf_nat", [P, NT, FH], where=small)
            lf_pages = sb("lf_pages", [P, SB * NPAGE, FH], where=small)
            knat = rows

            w_in = [sem(f"fw_in{s}") for s in range(3)]
            wf_in = sem("fwf_in")
            q_done, k_done, q_kept, k_kept = sem("fq_done"), sem("fk_done"), sem("fq_kept"), sem("fk_kept")
            v_done, v_kept, f_done = sem("fv_done"), sem("fv_kept"), sem("ff_done")
            kn_done, kn_kept, kv_out = sem("fkn_done"), sem("fkn_kept"), sem("fkv_out")
            pages_in, past_in, past_turned = sem("pages_in"), lasting("past_in"), sem("past_turned")
            bent, rounded, logged, lf_ready = sem("f_bent"), sem("f_rounded"), sem("f_logged"), sem("f_lf")
            lf_turned, lf_natural, negc_ready, negc_out = sem("lf_turned"), sem("lf_natural"), sem("negc_ready"), sem("negc_out")
            ch_dve = sem("fox_own_dve")
            w_view = i["fox_w_in"][0].rearrange("(p c) n -> p c n", c=KC)

            def sp_(sp):
                sp.dma_start(wf[:], w_view[:, :, 3 * D:3 * D + FH]).then_inc(wf_in, 16)
                sp.dma_start(bf[:], i["fox_b_f"].rearrange("a h -> h a")).then_inc(wf_in, 16)
                sp.dma_start(pages[:], i["page_table"].rearrange("(o b) n -> o (b n)", o=1)).then_inc(pages_in, 16)
                for blk in range(6):
                    if blk >= 3:
                        sp.wait_ge(q_done if blk < 5 else k_done, 8 if blk == 4 else 4)
                    sp.dma_start(wblk[:, blk % 3], w_view[:, :, blk * 512:blk * 512 + 512]).then_inc(w_in[blk % 3], 16)
                sp.wait_ge(v_kept, 2 * NT)
                for dst, src in ((("v_prompt", "v_sample"), v), (("k_prompt", "k_sample"), knat)):
                    if src is knat:
                        sp.wait_ge(kn_kept, NT)
                    sp.dma_start(o[dst[0]].rearrange("a b (n p) h d -> p (a b n) (h d)", p=P),
                                 src[:, 0:NT - 1, :]).then_inc(kv_out, 16)
                    sp.dma_start(o[dst[1]].rearrange("a b s h d -> (a b s) (h d)"),
                                 src[0:SAMP, NT - 1, :]).then_inc(kv_out, 16)
                sp.wait_ge(lf_natural, 2)
                sp.dma_start(o["logf_prompt"].rearrange("a b (n p) h -> p (a b n) h", p=P),
                             lf_nat[:, 0:NT - 1, :]).then_inc(kv_out, 16)
                sp.dma_start(o["logf_sample"].rearrange("a b s h -> (a b s) h"),
                             lf_nat[0:SAMP, NT - 1, :]).then_inc(kv_out, 16)
                sp.wait_ge(negc_ready, 1)
                sp.dma_start(negc_dram, negp[:]).then_inc(negc_out, 16)
                sp.wait_ge(negc_out, 16)
                sp.wait_ge(kv_out, 96)

            def pool_(pool):
                pool.wait_ge(pages_in, 16)
                with pool.Fori(0, SB * NPAGE) as n:
                    page = pool.value_load(pages[0:1, bass.ds(n, 1)], min_val=0, max_val=i["cache_logf"].shape[1] - 1)
                    pool.dma_start(lf_pages[:, bass.ds(n, 1), :],
                                   i["cache_logf"][0, bass.ds(page, 1)].rearrange("a p h -> p a h")).then_inc(past_in, 16)

            def pe_(pe):
                for blk in range(4):
                    pe.wait_ge(w_in[blk % 3], 16 * (blk // 3 + 1))
                    for cc in range(4):
                        g = blk * 4 + cc
                        if g >= 4:
                            pe.wait_ge(q_kept if g - 4 < 8 else k_kept, (g - 4) % 8 + 1)
                        for c in range(KC):
                            for a, b in ((0, PROMPT), (PROMPT, TOK)):
                                mm = pe.matmul(ps2[:, g % 4, a:b], wblk[:, blk % 3, c, cc * P:(cc + 1) * P],
                                               turned[:, c, a:b], start=(c == 0), stop=(c == KC - 1))
                        mm.then_inc(q_done if g < 8 else k_done, 1)
                pe.wait_ge(k_kept, 8)
                for blk in range(4, 6):
                    pe.wait_ge(w_in[blk % 3], 16 * (blk // 3 + 1))
                    for n, r in enumerate(ROWS):
                        m = (blk - 4) * NT + n
                        if m >= 8:
                            pe.wait_ge(v_kept, m - 7)
                        for c in range(KC):
                            mm = pe.matmul(ps[0:r, m % 8, :], turned[:, c, n * P:n * P + r], wblk[:, blk % 3, c, :],
                                           start=(c == 0), stop=(c == KC - 1))
                        mm.then_inc(v_done, 1)
                pe.wait_ge(wf_in, 32)
                pe.wait_ge(v_kept, 4)
                for c in range(KC):
                    for a, b in ((0, PROMPT), (PROMPT, TOK)):
                        mm = pe.matmul(ps2[0:FH, 1, a:b], wf[:, c, :], turned[:, c, a:b],
                                       start=(c == 0), stop=(c == KC - 1))
                mm.then_inc(f_done, 1)
                pe.wait_ge(v_kept, 2 * NT)
                for n, r in enumerate(ROWS):
                    if n >= 2:
                        pe.wait_ge(kn_kept, n - 1)
                    for p in range(PAIRS):
                        mm = pe.transpose(ps2[0:r, 2 + n % 2, p * P:(p + 1) * P], kT[:, p, n * P:n * P + r], ident)
                    mm.then_inc(kn_done, 1)
                pe.wait_ge(lf_ready, 1)
                for n, r in enumerate(ROWS):
                    mm = pe.transpose(ps[0:r, 2, n * FH:(n + 1) * FH], lf[:, n * P:n * P + r], ident[0:FH, 0:FH])
                mm.then_inc(lf_turned, 1)
                pe.wait_ge(past_in, 16 * SB * NPAGE)
                pe.wait_ge(kn_kept, NT)
                for b in range(SB):
                    if b == 2:
                        pe.wait_ge(lf_natural, 2)
                    for g in range(NPAGE):
                        mm = pe.transpose(ps[0:FH, b, g * P:(g + 1) * P], lf_pages[:, b * NPAGE + g, :], ident)
                    mm.then_inc(past_turned, 1)

            def act_(act):
                for g in range(8):
                    act.wait_ge(q_done, g + 1)
                    act.activation(qT[:, g, :], ps2[:, g % 4, 0:TOK], ACT.Copy, scale=FD ** -0.5).then_inc(q_kept, 1)
                for m in range(2 * NT):
                    act.wait_ge(v_done, m + 1)
                    n = m % NT
                    act.activation(v[0:ROWS[n], n, (m // NT) * 512:(m // NT) * 512 + 512],
                                   ps[0:ROWS[n], m % 8, :], ACT.Copy).then_inc(v_kept, 1)
                log_sigmoid_act(act, neg_abs, e, u, lnu, bent, rounded, logged)

            def dve_(dve):
                ch = Chain(dve, ch_dve)
                ch.step(dve.memset(negc[:], 0.0))
                ch.step(dve.memset(v[SAMP:P, NT - 1, :], 0.0))
                for g in range(8):
                    dve.wait_ge(k_done, g + 1)
                    dve.tensor_copy(kT[:, g, :], ps2[:, g % 4, 0:TOK]).then_inc(k_kept, 1)
                dve.wait_ge(f_done, 1)
                ch(dve.tensor_scalar(z, ps2[0:FH, 1, 0:TOK], bf[:, 0:1], None, ALU.add))
                log_sigmoid_dve(dve, ch, lf[:], z, neg_abs, e, u, lnu, bent, rounded, logged)
                dve.sem_inc(lf_ready, 1)
                dve.tensor_tensor_scan(negp[:], const("ones", FH)[:, 0:PROMPT], lf[:, 0:PROMPT], 0.0,
                                       ALU.mult, ALU.subtract).then_inc(negc_ready, 1)
                ch.step(dve.tensor_copy(lfs[:, :, PAST:], lf[:, PROMPT:TOK].rearrange("h (b s) -> h b s", s=SS)))
                for n, r in enumerate(ROWS):
                    dve.wait_ge(kn_done, n + 1)
                    dve.tensor_copy(knat[0:r, n, :], ps2[0:r, 2 + n % 2, :]).then_inc(kn_kept, 1)
                dve.wait_ge(lf_turned, 1)
                dve.tensor_copy(lf_nat[:, 0:NT - 1, :], ps[:, 2, 0:(NT - 1) * FH].rearrange("p (n h) -> p n h", h=FH)
                                ).then_inc(lf_natural, 1)
                dve.tensor_copy(lf_nat[0:SAMP, NT - 1, :], ps[0:SAMP, 2, (NT - 1) * FH:NT * FH]).then_inc(lf_natural, 1)
                for b in range(SB):
                    dve.wait_ge(past_turned, b + 1)
                    ch(dve.tensor_copy(lfs[:, b, 0:PAST], ps[0:FH, b, :]))
                    ch.step(dve.tensor_tensor_scan(negc[0:FH, b, :], const("ones", FH), lfs[:, b, :], 0.0,
                                                   ALU.mult, ALU.subtract))
                ch.wait()

            phases.append(dict(sp=sp_, pool=pool_, pe=pe_, act=act_, dve=dve_))
            small.close()

            prompt_attention(qT, kT, v, negc)
            sample_attention(qT, kT, v, negc, pages)
            fx.close()
            with ExitStack() as wo:
                project_out("fox_out", i["fox_w_out"][0], NT - 1, wo)

        def prompt_attention(qT, kT, v, negc):
            pa = ExitStack()
            QT_ = NT - 1
            STEPS = 2 * QT_
            o_nat = rows
            qz = sb("qz", [P, 2, PROMPT], where=pa)
            bias = sb("bias", [P, 2, PROMPT], where=pa)
            bias_m = sb("bias_m", [P, 2, PROMPT], where=pa)
            sc = sb("sc", [P, 3, PROMPT], where=pa)
            pT = sb("pT", [P, 2, PROMPT], where=pa)
            m0 = sb("m0", [P, STEPS], where=pa)
            m1 = sb("m1", [P, STEPS], where=pa)
            negm = sb("negm", [P, STEPS], where=pa)
            rsum = sb("rsum", [P, STEPS], where=pa)
            rinv = sb("rinv", [P, STEPS], where=pa)
            qz_zero, qz_ready = sem("qz_zero"), sem("qz_ready")
            filled = sem("filled")
            bias_in, biasm_ready, bias_free = sem("bias_in"), sem("biasm_ready"), sem("bias_free")
            s_done, m_ready, p_ready, t_done = sem("pa_s_done"), sem("pa_m_ready"), sem("pa_p_ready"), sem("pa_t_done")
            t_kept, o_done, o_kept, own = sem("pa_t_kept"), sem("pa_o_done"), sem("pa_o_kept"), sem("pa_own")
            OWN = 3 * STEPS - 2

            def sp_(sp):
                with sp.Fori(FULL, TILES) as k:
                    sp.dma_start(y_dram[bass.ds(k * SLOT, SLOT), :],
                                 negc[P - SLOT:P].rearrange("p b t -> p (b t)")[:, 0:D]).then_inc(filled, 16)
                with sp.Fori(0, PAIRS) as p:
                    sp.wait_ge(bias_free, p + 1)
                    alone(sp)
                    for h in range(2):
                        sp.dma_start(bias[:, h, :], negc_dram[bass.ds(2 * p + h, 1), :].broadcast_to([P, PROMPT])
                                     ).then_inc(bias_in, 16)
                    sp.wait_ge(bias_in, 32 * p + 32)
                    alone(sp)
                sp.wait_ge(filled, 16 * (TILES - FULL))

            def pool_(pool):
                pool.memset(qz[:], 0.0).then_inc(qz_zero, 1)
                pool.wait_ge(qz_zero, 1)
                with pool.Fori(0, PAIRS) as p:
                    pool.wait_ge(o_done, p * STEPS + 1)
                    for h in range(2):
                        r = slice(h * FD, (h + 1) * FD)
                        pool.tensor_copy(qz[r, h, :], qT[r, bass.ds(p, 1), 0:PROMPT].rearrange("d a t -> d (a t)")
                                         ).then_inc(qz_ready, 1)
                    pool.wait_ge(bias_in, 32 * p + 32)
                    pool.wait_ge(qz_ready, 2 * p + 2)
                    pool.tensor_tensor(bias_m[:].rearrange("p h (n k) -> p (h n) k", k=P),
                                       bias[:].rearrange("p h (n k) -> p (h n) k", k=P),
                                       const("neg_causal").unsqueeze(1).broadcast_to([P, 2 * QT_, P]), ALU.add
                                       ).then_inc(biasm_ready, 1)

            def pe_(pe):
                pe.sem_inc(o_done, 1)
                with pe.Fori(0, PAIRS) as p:
                    def scores(st):
                        h, t = divmod(st, QT_)
                        if st == 0:
                            pe.wait_ge(qz_ready, 2 * p + 2)
                        pe.wait_ge(m_ready, p * STEPS + st + 1)
                        mm = pe.matmul(ps[:, st % 3, 0:(t + 1) * P], qz[:, h, t * P:(t + 1) * P],
                                       kT[:, bass.ds(p, 1), 0:(t + 1) * P].rearrange("d a t -> d (a t)"), start=True, stop=True)
                        mm.then_inc(s_done, 1)

                    def turn(st):
                        t = st % QT_
                        pe.wait_ge(p_ready, p * STEPS + st + 1)
                        pe.wait_ge(t_kept, p * STEPS + st + 1)
                        for k in range(t + 1):
                            mm = pe.transpose(ps[:, 3 + st % 2, k * P:(k + 1) * P], sc[:, st % 3, k * P:(k + 1) * P], ident)
                        mm.then_inc(t_done, 1)

                    def values(st):
                        h, t = divmod(st, QT_)
                        pe.wait_ge(t_kept, p * STEPS + st + 3)
                        pe.wait_ge(o_kept, p * STEPS + st + 1)
                        for k in range(t + 1):
                            mm = pe.matmul(ps[:, 5 + st % 2, 0:FD], pT[:, st % 2, k * P:(k + 1) * P],
                                           v[:, k, bass.ds(p * P + h * FD, FD)], start=(k == 0), stop=(k == t))
                        mm.then_inc(o_done, 1)

                    for st in range(STEPS + 2):
                        if st < STEPS:
                            scores(st)
                        if 1 <= st <= STEPS:
                            turn(st - 1)
                        if st >= 2:
                            values(st - 2)

            def dve_(dve):
                dve.sem_inc(m_ready, 3)
                dve.sem_inc(bias_free, 1)
                with dve.Fori(0, PAIRS) as p:
                    ch = Chain(dve, own, p * OWN)

                    def maximum(st):
                        h, t = divmod(st, QT_)
                        if st == 0:
                            dve.wait_ge(biasm_ready, p + 1)
                        dve.wait_ge(s_done, p * STEPS + st + 1)
                        if st >= 3:
                            dve.wait_ge(t_done, p * STEPS + st - 2)
                        alone(dve)
                        own_block = slice(t * P, (t + 1) * P)
                        if t:
                            ch.step(dve.tensor_tensor_reduce(sc[:, st % 3, 0:t * P], ps[:, st % 3, 0:t * P], bias[:, h, 0:t * P],
                                                             1.0, NEG, ALU.add, ALU.max, m0[:, st:st + 1]))
                            ch.wait()
                            alone(dve)
                            ch(dve.tensor_tensor_reduce(sc[:, st % 3, own_block], ps[:, st % 3, own_block],
                                                        bias_m[:, h, own_block], 1.0, m0[:, st:st + 1], ALU.add, ALU.max,
                                                        m1[:, st:st + 1]))
                        else:
                            ch(dve.tensor_tensor_reduce(sc[:, st % 3, own_block], ps[:, st % 3, own_block],
                                                        bias_m[:, h, own_block], 1.0, NEG, ALU.add, ALU.max,
                                                        m1[:, st:st + 1]))
                        dve.tensor_scalar(negm[:, st:st + 1], m1[:, st:st + 1], -1.0, None, ALU.mult).then_inc(m_ready, 1)

                    def output(st):
                        h, t = divmod(st, QT_)
                        dve.wait_ge(p_ready, p * STEPS + st + 1)
                        ch(dve.reciprocal(rinv[:, st:st + 1], rsum[:, st:st + 1]))
                        dve.wait_ge(o_done, p * STEPS + st + 2)
                        ins = dve.tensor_scalar(o_nat[:, t, bass.ds(p * P + h * FD, FD)], ps[:, 5 + st % 2, 0:FD],
                                                rinv[:, st:st + 1], None, ALU.mult)
                        ins.then_inc(o_kept, 1)

                    for st in range(STEPS + 2):
                        if st < STEPS:
                            maximum(st)
                        if st >= 2:
                            output(st - 2)
                        if st == STEPS - 1:
                            dve.sem_inc(bias_free, 1)
                    assert ch.n == OWN

            def act_(act):
                act.sem_inc(t_kept, 2)
                act.sem_inc(o_kept, 2)
                with act.Fori(0, PAIRS) as p:
                    def soft(st):
                        t = st % QT_
                        act.wait_ge(m_ready, p * STEPS + st + 4)
                        act.activation(sc[:, st % 3, 0:(t + 1) * P], sc[:, st % 3, 0:(t + 1) * P], ACT.Exp,
                                       bias=negm[:, st:st + 1], accum_out=rsum[:, st:st + 1]).then_inc(p_ready, 1)

                    def keep(st):
                        t = st % QT_
                        act.wait_ge(t_done, p * STEPS + st + 1)
                        if st >= 2:
                            act.wait_ge(o_done, p * STEPS + st)
                        act.activation(pT[:, st % 2, 0:(t + 1) * P], ps[:, 3 + st % 2, 0:(t + 1) * P], ACT.Copy
                                       ).then_inc(t_kept, 1)

                    for st in range(STEPS + 1):
                        if st < STEPS:
                            soft(st)
                        if st >= 1:
                            keep(st - 1)

            phases.append(dict(sp=sp_, pool=pool_, pe=pe_, act=act_, dve=dve_))
            pa.close()

        def sample_attention(qT, kT, v, negc, pages):
            da = ExitStack()
            kpg = sb("kpg", [P, NPAGE, D], where=da)
            vpg = sb("vpg", [P, 2, NPAGE, D], where=da)
            KT_ = turned[:, :, 0:PAST]
            qbd = sb("qbd", [P, PAIRS, P], where=da)
            pr = sb("pr", [P, PAST + SAMP], where=da)
            prT = sb("prT", [P, NPAGE + 1, P], where=da)
            mm_ = sb("dmax", [P, 4], where=da)
            rs = sb("dsum", [P, 4], where=da)
            k_in, v_in = sem("dk_in"), [sem("dv_in0"), sem("dv_in1")]
            kt_done, kt_kept_a, kt_kept_v = sem("dkt_done"), sem("dkt_kept_a"), sem("dkt_kept_v")
            q_ready, s_done, neg_ready = sem("dq_ready"), sem("ds_done"), sem("dneg_ready")
            p_exp, p_ready, t_done = sem("dp_exp"), sem("dp_ready"), sem("dt_done")
            pt_kept, o_done, o_kept, own, zero_d = sem("dpt_kept"), sem("do_done"), sem("do_kept"), sem("d_own"), sem("d_zero")

            def sp_(sp):
                with sp.Fori(0, SB // 2) as j:
                    for s in range(2):
                        b = 2 * j + s
                        sp.wait_ge(kt_done, PAIRS * b + 1)
                        alone(sp)
                        for g in range(NPAGE):
                            page = sp.value_load(pages[0:1, bass.ds(NPAGE * b + g, 1)], min_val=0,
                                                 max_val=i["cache_k"].shape[1] - 1)
                            sp.dma_start(kpg[:, g, :], i["cache_k"][0, bass.ds(page, 1)].rearrange("a p h d -> p (a h d)")
                                         ).then_inc(k_in, 16)
                        sp.wait_ge(o_done, b + 1)
                        alone(sp)
                        for g in range(NPAGE):
                            page = sp.value_load(pages[0:1, bass.ds(NPAGE * b + g, 1)], min_val=0,
                                                 max_val=i["cache_k"].shape[1] - 1)
                            sp.dma_start(vpg[:, s, g, :], i["cache_v"][0, bass.ds(page, 1)].rearrange("a p h d -> p (a h d)")
                                         ).then_inc(v_in[s], 16)

            def pe_(pe):
                pe.sem_inc(kt_done, 1)
                pe.sem_inc(o_done, 2)
                with pe.Fori(0, SB // 2) as j:
                    for s in range(2):
                        b = 2 * j + s
                        pe.wait_ge(k_in, 64 * b + 64)
                        for p in range(PAIRS):
                            pe.wait_ge((kt_kept_a, kt_kept_v)[p % 2], 4 * b + p // 2 + 1)
                            for g in range(NPAGE):
                                mm = pe.transpose(ps[:, p % 4, g * P:(g + 1) * P], kpg[:, g, p * P:(p + 1) * P], ident)
                            mm.then_inc(kt_done, 1)
                        pe.wait_ge(q_ready, 2 * b + 2)
                        pe.wait_ge(p_exp, 2 * b + 2)
                        pe.wait_ge(o_kept, 2 * b + 2)
                        pe.wait_ge(kt_kept_a, 4 * b + 6)
                        pe.wait_ge(kt_kept_v, 4 * b + 6)
                        for p in range(PAIRS):
                            pe.matmul(ps[:, 4, :], qbd[:, p, :], KT_[:, p, :], start=(p == 0), stop=False)
                        pe.matmul(ps[:, 4, :], const("head_rows"), negc[:, bass.ds(b, 1), 0:PAST].rearrange("h a t -> h (a t)"),
                                  start=False, stop=True)
                        for p in range(PAIRS):
                            pe.matmul(ps[:, 5, 0:SAMP], qbd[:, p, :], kT[:, p, PROMPT:TOK], start=(p == 0), stop=False)
                        pe.matmul(ps[:, 5, 0:SAMP], const("head_rows"), negc[:, :, PAST:PAST + SS], start=False, stop=False)
                        pe.matmul(ps[:, 5, 0:SAMP], ident, const("dec_mask")[:, bass.ds(b * SAMP, SAMP)],
                                  start=False, stop=True).then_inc(s_done, 1)
                        pe.wait_ge(p_ready, b + 1)
                        for g in range(NPAGE):
                            pe.transpose(ps[:, 6, g * P:(g + 1) * P], pr[:, g * P:(g + 1) * P], ident)
                        pe.transpose(ps[0:SAMP, 7, 0:P], pr[:, PAST:PAST + SAMP], ident).then_inc(t_done, 1)
                        pe.wait_ge(pt_kept, 2 * b + 2)
                        pe.wait_ge(v_in[s], 64 * j + 64)
                        for p in range(PAIRS):
                            out = ps[:, 5, 64 + p * 2 * SS:64 + (p + 1) * 2 * SS]
                            for g in range(NPAGE):
                                pe.matmul(out, vpg[:, s, g, p * P:(p + 1) * P], prT[:, g, p * 2 * SS:(p + 1) * 2 * SS],
                                          start=(g == 0), stop=False)
                            mm = pe.matmul(out, v[:, NT - 1, p * P:(p + 1) * P],
                                           prT[:, NPAGE, p * 2 * SS:(p + 1) * 2 * SS], start=False, stop=True)
                        mm.then_inc(o_done, 1)

            def act_(act):
                act.sem_inc(kt_kept_a, 2)
                act.sem_inc(p_exp, 2)
                with act.Fori(0, SB // 2) as j:
                    for s in range(2):
                        b = 2 * j + s
                        for p in range(0, PAIRS, 2):
                            act.wait_ge(kt_done, PAIRS * b + p + 2)
                            if p == 0:
                                act.wait_ge(o_kept, 2 * b + 2)
                            act.activation(KT_[:, p, :], ps[:, p % 4, :], ACT.Copy).then_inc(kt_kept_a, 1)
                        act.wait_ge(neg_ready, b + 1)
                        act.activation(pr[:, 0:PAST], ps[:, 4, :], ACT.Exp, bias=mm_[:, 3:4],
                                       accum_out=rs[:, 0:1]).then_inc(p_exp, 1)
                        act.activation(pr[:, PAST:], ps[:, 5, 0:SAMP], ACT.Exp, bias=mm_[:, 3:4],
                                       accum_out=rs[:, 1:2]).then_inc(p_exp, 1)
                        act.wait_ge(t_done, b + 1)
                        act.activation(prT[:, 0:NPAGE, :], ps[:, 6, :].rearrange("p (g q) -> p g q", q=P), ACT.Copy
                                       ).then_inc(pt_kept, 1)

            def dve_(dve):
                dve.memset(qbd[:], 0.0).then_inc(zero_d, 1)
                dve.memset(prT[SAMP:P, NPAGE, :], 0.0).then_inc(zero_d, 1)
                dve.wait_ge(zero_d, 2)
                dve.sem_inc(kt_kept_v, 2)
                dve.sem_inc(o_kept, 2)
                OWN_D = 5
                with dve.Fori(0, SB // 2) as j:
                    for s in range(2):
                        b = 2 * j + s
                        ch = Chain(dve, own, b * OWN_D)
                        for h in range(2):
                            r = slice(h * FD, (h + 1) * FD)
                            src = qT[r, :, bass.ds(PROMPT + b * SS, SS)]
                            dst = qbd[r].rearrange("d p c -> d (p c)")[:, h * SS:h * SS + (PAIRS - 1) * (P + 2 * SS) + SS]
                            dst = bass.AP(dst.tensor, dst.offset, [dst.ap[0], [P + 2 * SS, PAIRS], [1, SS]])
                            dve.tensor_copy(dst, src).then_inc(q_ready, 1)
                        for p in range(1, PAIRS, 2):
                            dve.wait_ge(kt_done, PAIRS * b + p + 2)
                            dve.tensor_copy(KT_[:, p, :], ps[:, p % 4, :]).then_inc(kt_kept_v, 1)
                        dve.wait_ge(s_done, b + 1)
                        ch.step(dve.tensor_reduce(mm_[:, 0:1], ps[:, 4, :], AX, ALU.max))
                        ch(dve.tensor_reduce(mm_[:, 1:2], ps[:, 5, 0:SAMP], AX, ALU.max))
                        ch(dve.tensor_tensor(mm_[:, 2:3], mm_[:, 0:1], mm_[:, 1:2], ALU.max))
                        dve.tensor_scalar(mm_[:, 3:4], mm_[:, 2:3], -1.0, None, ALU.mult).then_inc(neg_ready, 1)
                        dve.wait_ge(p_exp, 2 * b + 4)
                        ch(dve.tensor_tensor(rs[:, 2:3], rs[:, 0:1], rs[:, 1:2], ALU.add))
                        ch(dve.reciprocal(rs[:, 3:4], rs[:, 2:3]))
                        dve.tensor_scalar(pr[:], pr[:], rs[:, 3:4], None, ALU.mult).then_inc(p_ready, 1)
                        dve.wait_ge(t_done, b + 1)
                        dve.tensor_copy(prT[0:SAMP, NPAGE, :], ps[0:SAMP, 7, 0:P]).then_inc(pt_kept, 1)
                        dve.wait_ge(o_done, b + 3)
                        for h in range(2):
                            r = slice(h * FD, (h + 1) * FD)
                            dve.tensor_copy(turned[r, :, bass.ds(PROMPT + b * SS, SS)],
                                            ps[r, 5, 64:64 + PAIRS * 2 * SS].rearrange("d (p h q) -> d p h q", h=2, q=SS)[:, :, h, :]
                                            ).then_inc(o_kept, 1)
                        assert ch.n == OWN_D

            phases.append(dict(sp=sp_, pe=pe_, act=act_, dve=dve_))
            da.close()

        def moe(layer):
            tag = f"moe{layer}_"
            gain = gains[:, 2 * layer + 1, :]
            norm(tag + "norm", gain, keep=h_dram[layer])
            mx = ExitStack()
            wr = sb(tag + "wr", [P, KC, LG], where=mx)
            lb = sb(tag + "lb", [P, LG], where=mx)
            lg = sb(tag + "lg", [P, NT, LG], where=mx)
            s5 = {n: sb(tag + n, [P, NT], where=mx) for n in ("gmax", "pg", "v1", "v2", "ex", "den", "w1", "w2", "top",
                                                              "t1", "t2", "r1", "r2", "sl")}
            g4 = {n: sb(tag + n, [P, NT, GROUPS], where=mx) for n in ("ga", "gb", "goh")}
            e32 = {n: sb(tag + n, [P, NT, EXP], where=mx) for n in ("en", "ea", "oh1", "oh2", "both", "rank", "fl", "tl", "md")}
            c32 = {n: sb(tag + n, [P, EXP], where=mx) for n in ("cnt", "nt", "end", "st")}
            slot = sb(tag + "slot", [P, 2, NT], U32, where=mx)
            rowsel = sb(tag + "rowsel", [P, 2 * NT, SLOT], where=mx)
            tilesel = sb(tag + "tilesel", [P, 2 * NT, TILES], where=mx)
            src_row = sb(tag + "src_row", [SLOT, TILES], U32, where=mx)
            et = sb(tag + "et", [1, TILES, EXP], where=mx)
            ef = sb(tag + "ef", [1, TILES + 1], where=mx)
            ctl = sb(tag + "ctl", [1, TILES + 1], I32, where=mx)
            wr_in, lg_done, own = sem(tag + "wr_in"), sem(tag + "lg_done"), sem(tag + "own")
            to_exp, exped = sem(tag + "to_exp"), sem(tag + "exped")
            both_ready, rank_done, sel_ready, src_done, routed = (sem(tag + "both"), sem(tag + "rank"), sem(tag + "sel"),
                                                                  sem(tag + "src"), sem(tag + "routed"))

            def sp_(sp):
                sp.dma_start(wr[:, :, 0:GROUPS], i["moe_w_group"][layer].rearrange("(p c) n -> p c n", c=KC)).then_inc(wr_in, 16)
                sp.dma_start(wr[:, :, GROUPS:], i["moe_w_router"][layer].rearrange("(p c) n -> p c n", c=KC)).then_inc(wr_in, 16)
                sp.dma_start(lb[:, 0:GROUPS], i["moe_b_group"][layer:layer + 1, :].broadcast_to([P, GROUPS])).then_inc(wr_in, 16)
                sp.dma_start(lb[:, GROUPS:], i["moe_b_router"][layer:layer + 1, :].broadcast_to([P, EXP])).then_inc(wr_in, 16)

            def pe_(pe):
                pe.wait_ge(wr_in, 64)
                for n, r in enumerate(ROWS):
                    for c in range(KC):
                        mm = pe.matmul(ps[0:r, 0, n * LG:(n + 1) * LG], turned[:, c, n * P:n * P + r], wr[:, c, :],
                                       start=(c == 0), stop=(c == KC - 1))
                mm.then_inc(lg_done, 1)
                pe.wait_ge(both_ready, 1)
                for n in range(NT):
                    for j in range(n + 1):
                        pe.matmul(ps[:, 1, n * EXP:(n + 1) * EXP], const("before") if j == n else const("ones")[:, 0:P],
                                  e32["both"][:, j, :], start=(j == 0), stop=(j == n))
                for n in range(NT):
                    mm = pe.matmul(ps[:, 1, NT * EXP:(NT + 1) * EXP], const("ones")[:, 0:P], e32["both"][:, n, :],
                                   start=(n == 0), stop=(n == NT - 1))
                mm.then_inc(rank_done, 1)
                pe.wait_ge(sel_ready, 1)
                for k in range(2 * NT):
                    mm = pe.matmul(ps[0:SLOT, 2, 0:TILES], rowsel[:, k, :], tilesel[:, k, :], start=(k == 0), stop=(k == 2 * NT - 1))
                mm.then_inc(src_done, 1)

            def act_(act):
                act.wait_ge(to_exp, 1)
                act.activation(g4["gb"][:], g4["gb"][:], ACT.Exp).then_inc(exped, 1)
                act.wait_ge(to_exp, 2)
                act.activation(s5["ex"][:], s5["ex"][:], ACT.Exp).then_inc(exped, 1)

            def dve_(dve):
                ch = Chain(dve, own)

                def wide(ap, n):
                    return ap.unsqueeze(2).broadcast_to([P, NT, n])

                def first_max(oh, val, top, scratch, rev, n):
                    ch(dve.tensor_reduce(top, val, AX, ALU.max))
                    ch(dve.tensor_tensor(scratch, val, wide(top, n), ALU.is_ge))
                    ch(dve.tensor_tensor(scratch, scratch, rev.unsqueeze(1).broadcast_to([P, NT, n]), ALU.mult))
                    ch(dve.tensor_reduce(s5["top"][:], scratch, AX, ALU.max))
                    ch(dve.tensor_tensor(oh, scratch, wide(s5["top"][:], n), ALU.is_equal))

                ch(dve.memset(lg[:], 0.0))
                dve.wait_ge(lg_done, 1)
                ch.step(dve.tensor_tensor(lg[:, 0:NT - 1, :], ps[:, 0, 0:(NT - 1) * LG].rearrange("p (n e) -> p n e", e=LG),
                                          lb[:].unsqueeze(1).broadcast_to([P, NT - 1, LG]), ALU.add))
                ch(dve.tensor_tensor(lg[0:SAMP, NT - 1, :], ps[0:SAMP, 0, (NT - 1) * LG:NT * LG], lb[0:SAMP, :], ALU.add))
                g, ex = lg[:, :, 0:GROUPS], lg[:, :, GROUPS:]
                first_max(g4["goh"][:], g, s5["gmax"][:], g4["ga"][:], const("rev4"), GROUPS)
                ch(dve.tensor_tensor(g4["gb"][:], g, wide(s5["gmax"][:], GROUPS), ALU.subtract))
                dve.sem_inc(to_exp, 1)
                ch(dve.tensor_scalar(g4["ga"][:], g4["goh"][:], -1.0, -NEG, ALU.add, ALU.mult))
                en = e32["en"][:].rearrange("p n (g k) -> p n g k", k=PER)
                ch(dve.tensor_tensor(en, ex.rearrange("p n (g k) -> p n g k", k=PER),
                                     g4["goh"][:].unsqueeze(3).broadcast_to([P, NT, GROUPS, PER]), ALU.mult))
                ch(dve.tensor_tensor(en, en, g4["ga"][:].unsqueeze(3).broadcast_to([P, NT, GROUPS, PER]), ALU.add))
                first_max(e32["oh1"][:], e32["en"][:], s5["v1"][:], e32["ea"][:], const("rev32"), EXP)
                ch(dve.scalar_tensor_tensor(e32["en"][:], e32["oh1"][:], -3e38, e32["en"][:], ALU.mult, ALU.add))
                first_max(e32["oh2"][:], e32["en"][:], s5["v2"][:], e32["ea"][:], const("rev32"), EXP)
                ch(dve.tensor_tensor(s5["ex"][:], s5["v2"][:], s5["v1"][:], ALU.subtract))
                dve.sem_inc(to_exp, 1)
                valid = wide(const("valid"), EXP)
                ch.step(dve.tensor_tensor(e32["oh1"][:], e32["oh1"][:], valid, ALU.mult))
                ch(dve.tensor_tensor(e32["oh2"][:], e32["oh2"][:], valid, ALU.mult))
                ch(dve.tensor_tensor(e32["both"][:], e32["oh1"][:], e32["oh2"][:], ALU.add))
                dve.sem_inc(both_ready, 1)
                dve.wait_ge(exped, 2)
                ch.step(dve.tensor_reduce(s5["pg"][:], g4["gb"][:], AX, ALU.add))
                ch(dve.tensor_scalar(s5["den"][:], s5["ex"][:], 1.0, None, ALU.add))
                ch(dve.tensor_tensor(s5["den"][:], s5["den"][:], s5["pg"][:], ALU.mult))
                ch(dve.reciprocal(s5["w1"][:], s5["den"][:]))
                ch(dve.tensor_tensor(s5["w2"][:], s5["w1"][:], s5["ex"][:], ALU.mult))
                dve.wait_ge(rank_done, 1)
                ch.step(dve.tensor_copy(e32["rank"][:].rearrange("p n e -> p (n e)"), ps[:, 1, 0:NT * EXP]))
                ch(dve.tensor_copy(c32["cnt"][:], ps[:, 1, NT * EXP:(NT + 1) * EXP]))
                ch.step(dve.tensor_scalar(c32["nt"][:], c32["cnt"][:], 0.0, None, ALU.is_gt))
                ch(dve.tensor_scalar(e32["fl"][:], e32["rank"][:], float(SLOT), None, ALU.is_ge))
                for k in range(1, TOK // SLOT):
                    ch(dve.scalar_tensor_tensor(c32["nt"][:], c32["cnt"][:], float(k * SLOT), c32["nt"][:], ALU.is_gt, ALU.add))
                    if k >= 2:
                        ch(dve.scalar_tensor_tensor(e32["fl"][:], e32["rank"][:], float(k * SLOT), e32["fl"][:], ALU.is_ge, ALU.add))
                ch(dve.tensor_tensor_scan(c32["end"][:], const("ones")[:, 0:EXP], c32["nt"][:], 0.0, ALU.mult, ALU.add))
                ch(dve.tensor_tensor(c32["st"][:], c32["end"][:], c32["nt"][:], ALU.subtract))
                ch.step(dve.tensor_tensor(e32["tl"][:], e32["fl"][:], c32["st"][:].unsqueeze(1).broadcast_to([P, NT, EXP]), ALU.add))
                ch(dve.scalar_tensor_tensor(e32["md"][:], e32["fl"][:], -float(SLOT), e32["rank"][:], ALU.mult, ALU.add))
                for j, oh in enumerate(("oh1", "oh2")):
                    t, r = (("t1", "r1"), ("t2", "r2"))[j]
                    ch(dve.tensor_tensor(e32["ea"][:], e32["tl"][:], e32[oh][:], ALU.mult))
                    ch(dve.tensor_reduce(s5[t][:], e32["ea"][:], AX, ALU.add))
                    ch(dve.tensor_tensor(e32["ea"][:], e32["md"][:], e32[oh][:], ALU.mult))
                    ch(dve.tensor_reduce(s5[r][:], e32["ea"][:], AX, ALU.add))
                    ch(dve.scalar_tensor_tensor(s5["sl"][:], s5[t][:], float(SLOT), s5[r][:], ALU.mult, ALU.add))
                    ch(dve.tensor_copy(slot[:, j, :], s5["sl"][:]))
                    for n in range(NT):
                        k = j * NT + n
                        ch.step(dve.tensor_scalar(rowsel[:, k, :], const("iota_slot"), s5[r][:, n:n + 1],
                                                  const("token")[:, n:n + 1], ALU.is_equal, ALU.mult))
                        ch.step(dve.tensor_scalar(tilesel[:, k, :], const("iota_tile"), s5[t][:, n:n + 1], None, ALU.is_equal))
                ch.wait()
                dve.sem_inc(sel_ready, 1)
                ch(dve.tensor_tensor(et[:], c32["end"][0:1, :].unsqueeze(1).broadcast_to([1, TILES, EXP]),
                                     const("iota_tile", 1).unsqueeze(2).broadcast_to([1, TILES, EXP]), ALU.is_le))
                ch.step(dve.tensor_reduce(ef[:, 0:TILES], et[:], AX, ALU.add))
                ch(dve.tensor_copy(ef[:, TILES:], c32["end"][0:1, EXP - 1:EXP]))
                ch(dve.tensor_scalar(ef[:, 0:TILES], ef[:, 0:TILES], float(EXP - 1), None, ALU.min))
                ch(dve.tensor_copy(ctl[:], ef[:]))
                dve.wait_ge(src_done, 1)
                ch(dve.tensor_copy(src_row[:], ps[0:SLOT, 2, 0:TILES]))

            phases.append(dict(sp=sp_, pe=pe_, act=act_, dve=dve_))

            wg = sb(tag + "wg", [P, RING, KC, HID], where=mx)
            wu = sb(tag + "wu", [P, RING, KC, HID], where=mx)
            wd = sb(tag + "wd", [P, RING, 2, D], where=mx)
            idx = sb(tag + "idx", [SLOT, RING], U32, where=mx)
            xg = sb(tag + "xg", [SLOT, RING, D], where=mx)
            xT = sb(tag + "xT", [P, RING, KC, SLOT], where=mx)
            sg = sb(tag + "sg", [P, RING, 2 * SLOT], where=mx)
            aT = sb(tag + "aT", [P, RING, 2 * SLOT], where=mx)
            y = sb(tag + "y", [SLOT, RING, D], where=mx)
            w_in = [sem(tag + f"w_in{u}") for u in range(RING)]
            x_in = [lasting(tag + f"x_in{u}") for u in range(RING)]
            y_out = [sem(tag + f"y_out{u}") for u in range(RING)]
            idx_ready, x_free = sem(tag + "idx_ready"), sem(tag + "x_free")
            xt_kept, gu_done, silu_done, a_ready, y_done = (sem(tag + "xt_kept"), sem(tag + "gu_done"), sem(tag + "silu"),
                                                            sem(tag + "a_ready"), sem(tag + "y_done"))
            y_kept_a, y_kept_v = sem(tag + "y_kept_a"), sem(tag + "y_kept_v")
            LOOPS = TILES // RING

            def used(eng):
                return eng.value_load(ctl[0:1, TILES:TILES + 1], min_val=1, max_val=TILES)

            def sp2(sp):
                live = used(sp)
                with sp.Fori(0, LOOPS) as j:
                    for s in range(RING):
                        k = RING * j + s
                        with sp.If(live > k):
                            e = sp.value_load(ctl[0:1, bass.ds(k, 1)], min_val=0, max_val=EXP - 1)
                            sp.wait_ge(y_done, k + 1)
                            for w, name, cc in ((wg, "moe_w_gate", KC), (wu, "moe_w_up", KC), (wd, "moe_w_down", 2)):
                                sp.dma_start(w[:, s], i[name][layer, bass.ds(e, 1)].rearrange("a (p c) n -> p (a c) n", c=cc)
                                             ).then_inc(w_in[s], 16)

            def pool2(pool):
                live = used(pool)
                with pool.Fori(0, LOOPS) as j:
                    for s in range(RING):
                        k = RING * j + s
                        with pool.If(live > k):
                            pool.wait_ge(x_free, k + 1)
                            pool.tensor_copy(idx[:, s:s + 1], src_row[:, bass.ds(k, 1)]).then_inc(idx_ready, 1)
                            pool.wait_ge(idx_ready, k + 1)
                            alone(pool)
                            pool.indirect_dma_start(xg[:, s, :], None, h_dram[layer],
                                                    bass.IndirectOffsetOnAxis(ap=idx[:, s:s + 1], axis=0)).then_inc(x_in[s], 16)

            def pe2(pe):
                pe.sem_inc(y_done, RING)
                pe.sem_inc(x_free, RING)
                live = used(pe)
                with pe.Fori(0, LOOPS) as j:
                    for s in range(RING):
                        k = RING * j + s
                        with pe.If(live > k):
                            pe.wait_ge(x_in[s], 16 * j + 16)
                            alone(pe)
                            for c in range(KC):
                                mm = pe.transpose(ps[:, s, c * SLOT:(c + 1) * SLOT], xg[:, s, c:D:KC], ident[0:SLOT, 0:SLOT])
                            mm.then_inc(x_free, 1)
                            pe.wait_ge(w_in[s], 48 * j + 48)
                            pe.wait_ge(xt_kept, k + 1)
                            for m in range(4):
                                w = (wg, wu)[m // 2]
                                for c in range(KC):
                                    mm = pe.matmul(ps[:, 3 + s, m * SLOT:(m + 1) * SLOT], w[:, s, c, m % 2:HID:2], xT[:, s, c, :],
                                                   start=(c == 0), stop=(c == KC - 1))
                            mm.then_inc(gu_done, 1)
                            pe.wait_ge(a_ready, k + 1)
                            pe.wait_ge(y_kept_a, k + 1)
                            pe.wait_ge(y_kept_v, k + 1)
                            for half in range(2):
                                for m in range(2):
                                    mm = pe.matmul(ps[0:SLOT, 6 + half, :], aT[:, s, m * SLOT:(m + 1) * SLOT],
                                                   wd[:, s, m, half * 512:half * 512 + 512], start=(m == 0), stop=(m == 1))
                            mm.then_inc(y_done, 1)

            def act2(act):
                act.sem_inc(y_kept_a, 1)
                for s in range(RING):
                    act.sem_inc(y_out[s], 16)
                live = used(act)
                with act.Fori(0, LOOPS) as j:
                    for s in range(RING):
                        k = RING * j + s
                        with act.If(live > k):
                            act.wait_ge(gu_done, k + 1)
                            act.activation(sg[:, s, :], ps[:, 3 + s, 0:2 * SLOT], ACT.Silu).then_inc(silu_done, 1)
                            act.wait_ge(y_done, k + 1 + RING)
                            act.wait_ge(y_out[s], 16 * j + 16)
                            act.activation(y[:, s, 0:512], ps[0:SLOT, 6, :], ACT.Copy).then_inc(y_kept_a, 1)
                            act.wait_ge(y_kept_a, k + 2)
                            act.wait_ge(y_kept_v, k + 2)
                            act.dma_start(y_dram[bass.ds(k * SLOT, SLOT), :], y[:, s, :]).then_inc(y_out[s], 16)
                        with act.If(live <= k):
                            act.sem_inc(y_out[s], 16)
                for s in range(RING):
                    act.wait_ge(y_out[s], 16 * (LOOPS + 1))

            def dve2(dve):
                dve.sem_inc(y_kept_v, 1)
                live = used(dve)
                with dve.Fori(0, LOOPS) as j:
                    for s in range(RING):
                        k = RING * j + s
                        with dve.If(live > k):
                            dve.wait_ge(x_free, k + 1 + RING)
                            dve.tensor_tensor(xT[:, s], ps[:, s, :].rearrange("p (c t) -> p c t", t=SLOT),
                                              gain.unsqueeze(2).broadcast_to([P, KC, SLOT]), ALU.mult).then_inc(xt_kept, 1)
                            dve.wait_ge(silu_done, k + 1)
                            dve.tensor_tensor(aT[:, s, :], sg[:, s, :], ps[:, 3 + s, 2 * SLOT:4 * SLOT], ALU.mult
                                              ).then_inc(a_ready, 1)
                            dve.wait_ge(y_done, k + 1 + RING)
                            dve.wait_ge(y_out[s], 16 * j + 16)
                            dve.tensor_copy(y[:, s, 512:1024], ps[0:SLOT, 7, :]).then_inc(y_kept_v, 1)

            phases.append(dict(sp=sp2, pool=pool2, pe=pe2, act=act2, dve=dve2))

            combined = sem(tag + "combined")
            yg_in = [lasting(tag + f"yg_in{u}") for u in range(4)]
            yg = wg[:].rearrange("p r c n -> p (r c n)")

            def pool3(pool):
                for k in range(2 * NT):
                    n, j = divmod(k, 2)
                    if k >= 4:
                        pool.wait_ge(combined, k - 3)
                    pool.indirect_dma_start(yg[0:ROWS[n], (k % 4) * D:(k % 4 + 1) * D], None, y_dram,
                                            bass.IndirectOffsetOnAxis(ap=slot[0:ROWS[n], j, n:n + 1], axis=0)
                                            ).then_inc(yg_in[k % 4], 16)

            def dve3(dve):
                for k in range(2 * NT):
                    n, j = divmod(k, 2)
                    r = ROWS[n]
                    dve.wait_ge(yg_in[k % 4], 16 * (k // 4 + 1))
                    if j:
                        dve.wait_ge(combined, k)
                    dve.scalar_tensor_tensor(x[0:r, n, :], yg[0:r, (k % 4) * D:(k % 4 + 1) * D],
                                             s5["w2" if j else "w1"][0:r, n:n + 1], x[0:r, n, :], ALU.mult, ALU.add
                                             ).then_inc(combined, 1)

            phases.append(dict(pool=pool3, dve=dve3))
            mx.close()

        def mlstm():
            norm("mlstm_norm", gains[:, 2, :])
            mx = ExitStack()
            qT = sb("mqT", [P, MPAIRS, TOK], where=mx)
            kT = sb("mkT", [P, MPAIRS, TOK], where=mx)
            knat = sb("mknat", [P, NT, MH * MK], where=mx)
            vaug = sb("vaug", [P, NT, MH, MV + 1], where=mx)
            og = sb("og", [P, NT, D], where=mx)
            nat = sb("nat", [P, NT, 4, MH], where=mx)
            carryb = sb("carryb", [P, MPAIRS, SB], where=mx)
            hnorm = sb("hnorm", [P, D], where=mx)
            negg_dram = nc.dram_tensor("negg_rows", (MH, TOK), F32, kind="Internal").ap()
            small = ExitStack()
            wblk = sb("mwblk", [P, 3, KC, 512], where=small)
            wg = sb("mwg", [P, KC, 2 * MH], where=small)
            bi = sb("mbi", [MH, 1], where=small)
            bf = sb("mbf", [MH, 1], where=small)
            m0T = sb("m0T", [MH, SB], where=small)
            mout = sb("mout", [MH, 1 + SB], where=small)
            z, neg_abs, e, u, lnu, lf, ii = (wblk[0:MH, 0].rearrange("p c n -> p (c n)")[:, n * TOK:(n + 1) * TOK]
                                             for n in range(7))
            bb, a, g, negg, m = (wblk[0:MH, 1].rearrange("p c n -> p (c n)")[:, n * TOK:(n + 1) * TOK] for n in range(5))
            EXW = 2 * TOK + SAMP + SB
            ex = wblk[0:MH, 2].rearrange("p c n -> p (c n)")[:, 0:EXW]
            enm, wk = ex[:, 0:TOK], ex[:, TOK:2 * TOK]
            wint, carry = ex[:, 2 * TOK:2 * TOK + SAMP], ex[:, 2 * TOK + SAMP:EXW]

            w_in = [sem(f"mw_in{s}") for s in range(3)]
            wg_in, hn_in = sem("mwg_in"), sem("mhn_in")
            q_done, k_done, q_kept, k_kept = sem("mq_done"), sem("mk_done"), sem("mq_kept"), sem("mk_kept")
            v_done, v_kept, o_done, o_kept = sem("mv_done"), sem("mv_kept"), sem("mo_done"), sem("mo_kept")
            g_done, kn_done, kn_kept = sem("mg_done"), sem("mkn_done"), sem("mkn_kept")
            bent, rounded, logged, own = sem("m_bent"), sem("m_rounded"), sem("m_logged"), sem("m_own")
            ex_ready, exped, nat_done, g_out, mout_ready = (sem("m_ex_ready"), sem("m_exped"), sem("m_nat_done"),
                                                            sem("m_g_out"), sem("m_out_ready"))
            w_view = i["mlstm_w_in"][0].rearrange("(p c) n -> p c n", c=KC)
            GATES = 2 * MH * MK + 2 * D

            def sp_(sp):
                sp.dma_start(wg[:], w_view[:, :, GATES:GATES + 2 * MH]).then_inc(wg_in, 16)
                sp.dma_start(bi[:], i["mlstm_b_i"].rearrange("a h -> h a")).then_inc(wg_in, 16)
                sp.dma_start(bf[:], i["mlstm_b_f"].rearrange("a h -> h a")).then_inc(wg_in, 16)
                sp.dma_start(m0T[:], i["state_m"][0].rearrange("b h -> h b"), allow_slow_non_contiguous=True).then_inc(wg_in, 16)
                for blk in range(6):
                    if blk >= 3:
                        sp.wait_ge((q_done, k_done, v_done)[blk - 3], (4, 4, NT)[blk - 3])
                    sp.dma_start(wblk[:, blk % 3], w_view[:, :, blk * 512:blk * 512 + 512]).then_inc(w_in[blk % 3], 16)
                sp.dma_start(hnorm[:], i["mlstm_head_norm"].rearrange("a h v -> a (h v)").broadcast_to([P, D])
                             ).then_inc(hn_in, 16)
                sp.wait_ge(mout_ready, 1)
                sp.dma_start(negg_dram, negg).then_inc(g_out, 16)
                sp.dma_start(o["m_prompt"].rearrange("a b h -> h (a b)"), mout[:, 0:1], allow_slow_non_contiguous=True).then_inc(g_out, 16)
                sp.dma_start(o["m_sample"].rearrange("a b h -> h (a b)"), mout[:, 1:], allow_slow_non_contiguous=True).then_inc(g_out, 16)
                sp.wait_ge(g_out, 48)
                sp.wait_ge(hn_in, 16)

            def pe_(pe):
                for blk in range(2):
                    pe.wait_ge(w_in[blk], 16)
                    for cc in range(4):
                        n = blk * 4 + cc
                        if n >= 4:
                            pe.wait_ge(q_kept, cc + 1)
                        for c in range(KC):
                            for lo, hi in ((0, PROMPT), (PROMPT, TOK)):
                                mm = pe.matmul(ps2[:, n % 4, lo:hi], wblk[:, blk, c, cc * P:(cc + 1) * P],
                                               turned[:, c, lo:hi], start=(c == 0), stop=(c == KC - 1))
                        mm.then_inc(k_done if blk else q_done, 1)
                pe.wait_ge(k_kept, 4)
                for blk in range(2, 6):
                    pe.wait_ge(w_in[blk % 3], 16 * (blk // 3 + 1))
                    for n, r in enumerate(ROWS):
                        k = (blk - 2) * NT + n
                        if k >= 8:
                            pe.wait_ge(v_kept if k - 8 < 2 * NT else o_kept, (k - 8) % (2 * NT) + 1)
                        for c in range(KC):
                            mm = pe.matmul(ps[0:r, k % 8, :], turned[:, c, n * P:n * P + r], wblk[:, blk % 3, c, :],
                                           start=(c == 0), stop=(c == KC - 1))
                        mm.then_inc(v_done if blk < 4 else o_done, 1)
                pe.wait_ge(wg_in, 64)
                pe.wait_ge(o_kept, 6)
                for gate in range(2):
                    for c in range(KC):
                        for lo, hi in ((0, PROMPT), (PROMPT, TOK)):
                            mm = pe.matmul(ps2[0:MH, 2 + gate, lo:hi], wg[:, c, gate * MH:(gate + 1) * MH],
                                           turned[:, c, lo:hi], start=(c == 0), stop=(c == KC - 1))
                mm.then_inc(g_done, 1)
                pe.wait_ge(o_kept, 2 * NT)
                for n, r in enumerate(ROWS):
                    if n >= 2:
                        pe.wait_ge(kn_kept, n - 1)
                    for p in range(MPAIRS):
                        mm = pe.transpose(ps[0:r, n % 2, p * P:(p + 1) * P], kT[:, p, n * P:n * P + r], ident)
                    mm.then_inc(kn_done, 1)
                pe.wait_ge(exped, 1)
                for n, r in enumerate(ROWS):
                    for k, src in enumerate((a, enm, wk)):
                        pe.transpose(ps[0:r, 2, (n * 4 + k) * MH:(n * 4 + k + 1) * MH], src[:, n * P:n * P + r], ident[0:MH, 0:MH])
                pe.transpose(ps[0:SAMP, 2, ((NT - 1) * 4 + 3) * MH:NT * 4 * MH], wint, ident[0:MH, 0:MH])
                for p in range(MPAIRS):
                    mm = pe.matmul(ps[:, 3, p * SB:(p + 1) * SB], const("selpair", MH)[:, p * P:(p + 1) * P], carry,
                                   start=True, stop=True)
                mm.then_inc(nat_done, 1)

            def act_(act):
                for n in range(4):
                    act.wait_ge(q_done, n + 1)
                    act.activation(qT[:, n, :], ps2[:, n, 0:TOK], ACT.Copy, scale=MK ** -0.5).then_inc(q_kept, 1)
                for k in range(2 * NT):
                    n, half = k % NT, k // NT
                    act.wait_ge(o_done, k + 1)
                    act.activation(og[0:ROWS[n], n, half * 512:half * 512 + 512], ps[0:ROWS[n], (k + 2 * NT) % 8, :],
                                   ACT.Sigmoid).then_inc(o_kept, 1)
                for n, r in enumerate(ROWS):
                    act.wait_ge(kn_done, n + 1)
                    act.activation(knat[0:r, n, :], ps[0:r, n % 2, :], ACT.Copy).then_inc(kn_kept, 1)
                log_sigmoid_act(act, neg_abs, e, u, lnu, bent, rounded, logged)
                act.wait_ge(ex_ready, 1)
                act.activation(ex, ex, ACT.Exp).then_inc(exped, 1)

            def dve_(dve):
                ch = Chain(dve, own)
                ch.step(dve.memset(vaug[:, :, :, MV:], 1.0))
                for n in range(4):
                    dve.wait_ge(k_done, n + 1)
                    dve.tensor_copy(kT[:, n, :], ps2[:, n, 0:TOK]).then_inc(k_kept, 1)
                for k in range(2 * NT):
                    n, half = k % NT, k // NT
                    dve.wait_ge(v_done, k + 1)
                    dve.tensor_copy(vaug[0:ROWS[n], n, half * 4:half * 4 + 4, 0:MV],
                                    ps[0:ROWS[n], k % 8, :].rearrange("p (h v) -> p h v", v=MV)).then_inc(v_kept, 1)
                dve.wait_ge(g_done, 1)
                ch.step(dve.tensor_scalar(ii, ps2[0:MH, 2, 0:TOK], bi[:, 0:1], None, ALU.add))
                ch(dve.tensor_scalar(z, ps2[0:MH, 3, 0:TOK], bf[:, 0:1], None, ALU.add))
                log_sigmoid_dve(dve, ch, lf, z, neg_abs, e, u, lnu, bent, rounded, logged)
                ones = const("ones", MH)

                def runs(ap):
                    return ap[:, PROMPT:TOK].rearrange("h (b s) -> h b s", s=SS)

                ch.step(dve.tensor_tensor_scan(bb[:, 0:PROMPT], ones[:, 0:PROMPT], lf[:, 0:PROMPT], 0.0, ALU.mult, ALU.add))
                for b in range(SB):
                    t = slice(PROMPT + b * SS, PROMPT + (b + 1) * SS)
                    ch.step(dve.tensor_tensor_scan(bb[:, t], ones[:, 0:SS], lf[:, t], 0.0, ALU.mult, ALU.add))
                ch.wait()
                ch(dve.tensor_tensor(a, ii, bb, ALU.subtract))
                ch.step(dve.tensor_tensor_scan(g[:, 0:PROMPT], ones[:, 0:PROMPT], a[:, 0:PROMPT], 0.0, ALU.mult, ALU.max))
                for b in range(SB):
                    t = slice(PROMPT + b * SS, PROMPT + (b + 1) * SS)
                    ch.step(dve.tensor_tensor_scan(g[:, t], ones[:, 0:SS], a[:, t], m0T[:, b:b + 1], ALU.mult, ALU.max))
                ch.wait()
                ch.step(dve.tensor_scalar(negg, g, -1.0, None, ALU.mult))
                ch(dve.tensor_tensor(m, bb, g, ALU.add))
                ch.step(dve.tensor_copy(mout[:, 0:1], m[:, PROMPT - 1:PROMPT]))
                ch(dve.tensor_copy(mout[:, 1:], runs(m)[:, :, SS - 1]))
                dve.sem_inc(mout_ready, 1)
                last = runs(g)[:, :, SS - 1:SS]
                ch.step(dve.tensor_scalar(enm, m, -1.0, None, ALU.mult))
                ch.step(dve.tensor_scalar(wk[:, 0:PROMPT], a[:, 0:PROMPT], g[:, PROMPT - 1:PROMPT], None, ALU.subtract))
                ch.step(dve.tensor_tensor(runs(wk), runs(a), last.broadcast_to([MH, SB, SS]), ALU.subtract))
                ch.step(dve.tensor_tensor(wint.rearrange("h (b s) -> h b s", s=SS), m0T[:].unsqueeze(2).broadcast_to([MH, SB, SS]),
                                          runs(g), ALU.subtract))
                ch(dve.tensor_tensor(carry, m0T[:], runs(g)[:, :, SS - 1], ALU.subtract))
                dve.sem_inc(ex_ready, 1)
                dve.wait_ge(nat_done, 1)
                ch.step(dve.tensor_copy(nat[:, 0:NT - 1, 0:3, :], ps[:, 2, 0:(NT - 1) * 4 * MH].rearrange(
                    "p (n k h) -> p n k h", k=4, h=MH)[:, :, 0:3, :]))
                ch.step(dve.tensor_copy(nat[0:SAMP, NT - 1, :, :], ps[0:SAMP, 2, (NT - 1) * 4 * MH:NT * 4 * MH].rearrange(
                    "p (k h) -> p k h", h=MH)))
                ch.step(dve.tensor_copy(carryb[:].rearrange("p c b -> p (c b)"), ps[:, 3, 0:MPAIRS * SB]))
                ch.wait()

            phases.append(dict(sp=sp_, pe=pe_, act=act_, dve=dve_))
            small.close()
            mlstm_prompt(qT, kT, knat, vaug, nat, negg_dram)
            mlstm_samples(qT, kT, knat, vaug, nat, carryb, negg_dram)
            head_norm(og, hnorm)
            mx.close()
            with ExitStack() as wo:
                project_out("mlstm_out", i["mlstm_w_out"][0], NT, wo)

        def mlstm_prompt(qT, kT, knat, vaug, nat, negg_dram):
            mp = ExitStack()
            KT = NT - 1
            STEPS = 2 * KT
            gb = sb("gb", [P, 2, PROMPT], where=mp)
            gm = sb("gm", [P, 2, PROMPT], where=mp)
            kz = sb("kz", [P, 2, PROMPT], where=mp)
            kw = sb("kw", [P, KT, P], where=mp)
            ew = sb("ew", [P, 2, PROMPT], where=mp)
            wt = sb("wt", [P, 2, KT, PROMPT], where=mp)
            cp = sb("cp", [P, MPAIRS, MV + 1], where=mp)
            dn = sb("dn", [P, 4, KT], where=mp)
            g_in, gm_ready, kz_ready, kw_ready = sem("mp_g_in"), sem("mp_gm"), sem("mp_kz"), sem("mp_kw")
            s_done, e_ready, w_ready, n_done = sem("mp_s_done"), sem("mp_e"), sem("mp_w"), sem("mp_n_done")
            h_kept, c_done, c_kept, own, zero = sem("mp_h_kept"), sem("mp_c_done"), sem("mp_c_kept"), sem("mp_own"), sem("mp_zero")
            c_out = sem("mp_c_out")
            OWN = 2 * 4

            def sp_(sp):
                with sp.Fori(0, MPAIRS) as p:
                    sp.wait_ge(e_ready, STEPS * p + 1)
                    alone(sp)
                    for h in range(2):
                        sp.dma_start(gb[:, h, :], negg_dram[bass.ds(2 * p + h, 1), 0:PROMPT].broadcast_to([P, PROMPT])
                                     ).then_inc(g_in, 16)
                sp.wait_ge(c_kept, 2 * MPAIRS + 2)
                sp.dma_start(o["C_prompt"].rearrange("a b (p h) d v -> (h d) (a b p) v", h=2), cp[:, :, 0:MV]).then_inc(c_out, 16)
                sp.dma_start(o["n_prompt"].rearrange("a b (p h) d -> (h d) (a b p)", h=2), cp[:, :, MV], allow_slow_non_contiguous=True).then_inc(c_out, 16)
                sp.wait_ge(c_out, 32)

            def pool_(pool):
                pool.memset(kz[:], 0.0).then_inc(zero, 1)
                pool.wait_ge(zero, 1)
                pool.sem_inc(kw_ready, 1)
                with pool.Fori(0, MPAIRS) as p:
                    pool.wait_ge(kw_ready, p + 1)
                    pool.wait_ge(s_done, STEPS * p + 1)
                    for h in range(2):
                        r = slice(h * MK, (h + 1) * MK)
                        pool.tensor_copy(kz[r, h, :], kT[r, bass.ds(p, 1), 0:PROMPT].rearrange("d a t -> d (a t)")
                                         ).then_inc(kz_ready, 1)
                    pool.wait_ge(kz_ready, 2 * p + 2)
                    pool.wait_ge(g_in, 32 * p + 32)
                    pool.tensor_tensor(gm[:].rearrange("p h (n k) -> p (h n) k", k=P), gb[:].rearrange("p h (n k) -> p (h n) k", k=P),
                                       const("neg_causal_t").unsqueeze(1).broadcast_to([P, 2 * KT, P]), ALU.add
                                       ).then_inc(gm_ready, 1)
                    pool.wait_ge(c_done, p + 1)
                    for h in range(2):
                        mm = pool.tensor_tensor(kw[:, :, h * MK:(h + 1) * MK], knat[:, 0:KT, bass.ds(p * P + h * MK, MK)],
                                                nat[:, 0:KT, 2, bass.ds(2 * p + h, 1)].broadcast_to([P, KT, MK]), ALU.mult)
                    mm.then_inc(kw_ready, 1)

            def pe_(pe):
                pe.sem_inc(s_done, 1)
                pe.sem_inc(n_done, 2)
                pe.sem_inc(c_done, 1)
                with pe.Fori(0, MPAIRS) as p:
                    def scores(st):
                        h, k = divmod(st, KT)
                        if st == 0:
                            pe.wait_ge(kz_ready, 2 * p + 2)
                        pe.wait_ge(w_ready, STEPS * p + st + 1)
                        pe.matmul(ps[:, st % 2, 0:PROMPT - k * P], kz[:, h, k * P:(k + 1) * P],
                                  qT[:, bass.ds(p, 1), k * P:PROMPT].rearrange("d a t -> d (a t)"), start=True, stop=True
                                  ).then_inc(s_done, 1)

                    def values(h):
                        pe.wait_ge(w_ready, STEPS * p + KT * h + KT + 2)
                        pe.wait_ge(h_kept, 2 * p + h + 1)
                        for t in range(KT):
                            for k in range(t + 1):
                                mm = pe.matmul(psf[:, 1024 * (1 + h) + 256 * t:1024 * (1 + h) + 256 * t + MV + 1],
                                               wt[:, h, k, t * P:(t + 1) * P],
                                               vaug[:, k, bass.ds(2 * p + h, 1), :].rearrange("s a v -> s (a v)"),
                                               start=(k == 0), stop=(k == t))
                        mm.then_inc(n_done, 1)

                    for st in range(STEPS):
                        scores(st)
                        if st == 5:
                            values(0)
                    values(1)
                    pe.wait_ge(kw_ready, p + 2)
                    pe.wait_ge(c_kept, 2 * p + 2)
                    for k in range(KT):
                        mm = pe.matmul(ps[:, 6, 0:2 * (MV + 1)], kw[:, k, :],
                                       vaug[:, k, bass.ds(2 * p, 2), :].rearrange("s h v -> s (h v)"),
                                       start=(k == 0), stop=(k == KT - 1))
                    mm.then_inc(c_done, 1)

            def act_(act):
                act.sem_inc(e_ready, 1)
                act.sem_inc(c_kept, 2)
                with act.Fori(0, MPAIRS) as p:
                    for st in range(STEPS):
                        h, k = divmod(st, KT)
                        if st == 0:
                            act.wait_ge(gm_ready, p + 1)
                        act.wait_ge(w_ready, STEPS * p + st + 1)
                        bias = nat[:, k, 0, bass.ds(2 * p + h, 1)]
                        ins = act.activation(ew[:, st % 2, k * P:(k + 1) * P], gm[:, h, k * P:(k + 1) * P], ACT.Exp, bias=bias)
                        if k < KT - 1:
                            ins = act.activation(ew[:, st % 2, (k + 1) * P:], gb[:, h, (k + 1) * P:], ACT.Exp, bias=bias)
                        ins.then_inc(e_ready, 1)
                    act.wait_ge(c_done, p + 2)
                    for h in range(2):
                        r = slice(h * MK, (h + 1) * MK)
                        act.activation(cp[r, bass.ds(p, 1), :].rearrange("d a v -> d (a v)"),
                                       ps[r, 6, h * (MV + 1):(h + 1) * (MV + 1)], ACT.Copy).then_inc(c_kept, 1)

            def dve_(dve):
                dve.sem_inc(w_ready, 2)
                dve.sem_inc(h_kept, 2)
                with dve.Fori(0, MPAIRS) as p:
                    ch = Chain(dve, own, p * OWN)

                    def weight(st):
                        h, k = divmod(st, KT)
                        dve.wait_ge(s_done, STEPS * p + st + 2)
                        dve.wait_ge(e_ready, STEPS * p + st + 2)
                        dve.wait_ge(n_done, 2 * p + h + 1)
                        dve.tensor_tensor(wt[:, h, k, k * P:], ew[:, st % 2, k * P:], ps[:, st % 2, 0:PROMPT - k * P], ALU.mult
                                          ).then_inc(w_ready, 1)

                    def heads(h):
                        num = psf[:, 1024 * (1 + h):1024 * (2 + h)].rearrange("p (t v) -> p t v", v=256)
                        dve.wait_ge(n_done, 2 * p + h + 3)
                        ch(dve.tensor_copy(dn[:, 0, :], num[:, :, MV]))
                        ch(dve.scalar_tensor_tensor(dn[:, 1, :], dn[:, 0, :], -1.0, dn[:, 0, :], ALU.mult, ALU.max))
                        ch(dve.tensor_tensor(dn[:, 2, :], dn[:, 1, :],
                                             nat[:, 0:KT, 1, bass.ds(2 * p + h, 1)].rearrange("p n a -> p (n a)"), ALU.max))
                        ch(dve.reciprocal(dn[:, 3, :], dn[:, 2, :]))
                        dve.tensor_tensor(rows[:, 0:KT, bass.ds(2 * p * MV + h * MV, MV)], num[:, :, 0:MV],
                                          dn[:, 3, :].unsqueeze(2).broadcast_to([P, KT, MV]), ALU.mult).then_inc(h_kept, 1)

                    for st in range(STEPS):
                        weight(st)
                        if st == 5:
                            heads(0)
                    dve.wait_ge(h_kept, 2 * p + 3)
                    heads(1)
                    assert ch.n == OWN

            phases.append(dict(sp=sp_, pool=pool_, pe=pe_, act=act_, dve=dve_))
            mp.close()

        def mlstm_samples(qT, kT, knat, vaug, nat, carryb, negg_dram):
            ms_ = ExitStack()
            C = sb("Cs", [P, SB, MPAIRS, MV + 1], where=ms_)
            qm = sb("qm", [P, MPAIRS, SB, SAMP], where=ms_)
            gs = sb("gs", [SAMP, MH, SAMP], where=ms_)
            ws = sb("ws", [SAMP, MH, SAMP], where=ms_)
            nd = sb("nd", [SAMP, MH, MV + 1], where=ms_)
            ni = sb("ni", [SAMP, MH, MV + 1], where=ms_)
            dn = sb("sdn", [SAMP, 3, MH], where=ms_)
            wkm = sb("wkm", [SAMP, SB, MH], where=ms_)
            kwm = sb("kwm", [SAMP, 2, MH * MK], where=ms_)
            c_in, gs_in, own = sem("sc_in"), sem("sgs_in"), sem("s_own")
            qm_ready, e_arg, e_ready, s_done = sem("s_qm"), sem("s_earg"), sem("s_e"), sem("s_s_done")
            w_ready, intra_done, inter_done, intra_kept = sem("s_w"), sem("s_intra"), sem("s_inter"), sem("s_intra_kept")
            inter_kept, carried, kwm_ready, dc_done, dc_added, c_out = (sem("s_inter_kept"), sem("s_carried"), sem("s_kwm"),
                                                                        sem("s_dc"), sem("s_dc_added"), sem("s_c_out"))
            R = slice(0, SAMP)
            L = NT - 1

            def sp_(sp):
                sp.dma_start(gs[:], negg_dram[:, PROMPT:TOK].unsqueeze(0).broadcast_to([SAMP, MH, SAMP])).then_inc(gs_in, 16)
                for b in range(SB):
                    sp.dma_start(C[:, b, :, 0:MV], i["state_C"][0, b].rearrange("(p h) d v -> (h d) p v", h=2)).then_inc(c_in, 16)
                    sp.dma_start(C[:, b, :, MV], i["state_n"][0, b].rearrange("(p h) d -> (h d) p", h=2), allow_slow_non_contiguous=True).then_inc(c_in, 16)
                for b in range(SB):
                    sp.wait_ge(dc_added, 2 * b + 2)
                    sp.dma_start(o["C_sample"][0, b].rearrange("(p h) d v -> (h d) p v", h=2), C[:, b, :, 0:MV]).then_inc(c_out, 16)
                    sp.dma_start(o["n_sample"][0, b].rearrange("(p h) d -> (h d) p", h=2), C[:, b, :, MV], allow_slow_non_contiguous=True).then_inc(c_out, 16)
                sp.wait_ge(c_out, 32 * SB)

            def pe_(pe):
                for h in range(MH):
                    r = slice((h % 2) * MK, (h % 2 + 1) * MK)
                    mm = pe.matmul(ps[R, h % 2, (h // 2) * SAMP:(h // 2 + 1) * SAMP], kT[r, h // 2, PROMPT:TOK],
                                   qT[r, h // 2, PROMPT:TOK], start=True, stop=True)
                mm.then_inc(s_done, 1)
                pe.wait_ge(w_ready, 2)
                for h in range(MH):
                    mm = pe.matmul(psf[R, 2048 + 256 * h:2048 + 256 * h + MV + 1], ws[:, h, :], vaug[R, L, h, :],
                                   start=True, stop=True)
                mm.then_inc(intra_done, 1)
                pe.wait_ge(c_in, 32 * SB)
                pe.wait_ge(qm_ready, MPAIRS)
                for h in range(MH):
                    r = slice((h % 2) * MK, (h % 2 + 1) * MK)
                    at = 1024 * (h % 2) + 256 * (h // 2)
                    for b in range(SB):
                        mm = pe.matmul(psf[R, at:at + MV + 1], qm[r, h // 2, b, :], C[r, b, h // 2, :],
                                       start=(b == 0), stop=(b == SB - 1))
                mm.then_inc(inter_done, 1)
                pe.wait_ge(intra_kept, 1)
                for b in range(SB):
                    pe.wait_ge(kwm_ready, b + 2)
                    if b:
                        pe.wait_ge(dc_added, 2 * b)
                    for p in range(MPAIRS):
                        mm = pe.matmul(ps[:, 4 + p, 0:2 * (MV + 1)], kwm[:, b % 2, p * P:(p + 1) * P],
                                       vaug[R, L, 2 * p:2 * p + 2, :].rearrange("s h v -> s (h v)"), start=True, stop=True)
                    mm.then_inc(dc_done, 1)

            def act_(act):
                act.wait_ge(e_arg, 1)
                act.activation(gs[:], gs[:], ACT.Exp).then_inc(e_ready, 1)
                act.wait_ge(intra_done, 1)
                act.activation(nd[:], psf[R, 2048:4096].rearrange("p (h v) -> p h v", v=256)[:, :, 0:MV + 1], ACT.Copy
                               ).then_inc(intra_kept, 1)

            def pool_(pool):
                pool.tensor_tensor(wkm[:], nat[R, L, 2, :].unsqueeze(1).broadcast_to([SAMP, SB, MH]),
                                   const("same", SAMP).unsqueeze(2).broadcast_to([SAMP, SB, MH]), ALU.mult).then_inc(kwm_ready, 1)
                pool.wait_ge(kwm_ready, 1)
                for b in range(SB):
                    if b >= 2:
                        pool.wait_ge(dc_done, b - 1)
                    pool.tensor_tensor(kwm[:, b % 2].rearrange("s (h d) -> s h d", d=MK),
                                       knat[R, L, :].rearrange("s (h d) -> s h d", d=MK),
                                       wkm[:, b, :].unsqueeze(2).broadcast_to([SAMP, MH, MK]), ALU.mult).then_inc(kwm_ready, 1)

            def dve_(dve):
                ch = Chain(dve, own)
                ch(dve.memset(qm[:], 0.0))
                for p in range(MPAIRS):
                    flat = qm[:, p].rearrange("d b t -> d (b t)")
                    dst = bass.AP(flat.tensor, flat.offset, [flat.ap[0], [SAMP + SS, SB], [1, SS]])
                    dve.tensor_copy(dst, qT[:, p, PROMPT:TOK].rearrange("d (b s) -> d b s", s=SS)).then_inc(qm_ready, 1)
                dve.wait_ge(gs_in, 16)
                ch(dve.tensor_tensor(gs[:], gs[:], const("samp_mask_t", SAMP).unsqueeze(1).broadcast_to([SAMP, MH, SAMP]), ALU.add))
                dve.tensor_tensor(gs[:], gs[:], nat[R, L, 0, :].unsqueeze(2).broadcast_to([SAMP, MH, SAMP]), ALU.add
                                  ).then_inc(e_arg, 1)
                dve.wait_ge(s_done, 1)
                dve.wait_ge(e_ready, 1)
                for u in range(2):
                    dve.tensor_tensor(ws[:, u:MH:2, :], gs[:, u:MH:2, :], ps[R, u, 0:MPAIRS * SAMP].rearrange("p (h t) -> p h t", t=SAMP),
                                      ALU.mult).then_inc(w_ready, 1)
                dve.wait_ge(inter_done, 1)
                for u in range(2):
                    ch.step(dve.tensor_tensor(ni[:, u:MH:2, :], psf[R, 1024 * u:1024 * (u + 1)].rearrange("p (h v) -> p h v", v=256)[:, :, 0:MV + 1],
                                              nat[R, L, 3, u:MH:2].unsqueeze(2).broadcast_to([SAMP, MPAIRS, MV + 1]), ALU.mult))
                dve.wait_ge(intra_kept, 1)
                ch.wait()
                ch(dve.tensor_tensor(nd[:], nd[:], ni[:], ALU.add))
                ch(dve.scalar_tensor_tensor(dn[:, 0, :], nd[:, :, MV], -1.0, nd[:, :, MV], ALU.mult, ALU.max))
                ch(dve.tensor_tensor(dn[:, 1, :], dn[:, 0, :], nat[R, L, 1, :], ALU.max))
                ch(dve.reciprocal(dn[:, 2, :], dn[:, 1, :]))
                ch(dve.tensor_tensor(rows[R, L, :].rearrange("p (h v) -> p h v", v=MV), nd[:, :, 0:MV],
                                     dn[:, 2, :].unsqueeze(2).broadcast_to([SAMP, MH, MV]), ALU.mult))
                for b in range(SB):
                    ch.step(dve.tensor_tensor(C[:, b], C[:, b], carryb[:, :, b:b + 1].broadcast_to([P, MPAIRS, MV + 1]), ALU.mult))
                ch.wait()
                for b in range(SB):
                    dve.wait_ge(dc_done, b + 1)
                    for u in range(2):
                        r = slice(u * MK, (u + 1) * MK)
                        dve.tensor_tensor(C[r, b], C[r, b], ps[r, 4:8, u * (MV + 1):(u + 1) * (MV + 1)], ALU.add
                                          ).then_inc(dc_added, 1)

            phases.append(dict(sp=sp_, pool=pool_, pe=pe_, act=act_, dve=dve_))
            ms_.close()

        def head_norm(og, hnorm):
            hs = ExitStack()
            tmp = sb("tmp", [P, 2, D], where=hs)
            hq = sb("hq", [P, NT, MH], where=hs)
            hr = sb("hr", [P, NT, MH], where=hs)
            squared, summed, rooted, own, gated = sem("h_squared"), sem("h_summed"), sem("h_rooted"), sem("h_own"), sem("h_gated")
            meaned = sem("h_meaned")

            def act_(act):
                for n, r in enumerate(ROWS):
                    if n >= 2:
                        act.wait_ge(summed, n)
                    act.activation(tmp[0:r, n % 2, :], rows[0:r, n, :], ACT.Square).then_inc(squared, 1)

            def pool_(pool):
                for n, r in enumerate(ROWS):
                    pool.tensor_tensor(og[0:r, n, :], og[0:r, n, :], hnorm[0:r, :], ALU.mult).then_inc(gated, 1)
                pool.wait_ge(gated, NT)
                pool.wait_ge(meaned, 1)
                pool.tensor_tensor(hr[:].rearrange("p n h -> p (n h)"), hq[:].rearrange("p n h -> p (n h)"),
                                   const("minus_half"), ALU.pow).then_inc(rooted, 1)

            def dve_(dve):
                ch = Chain(dve, own)
                dve.memset(hq[:], 1.0).then_inc(summed, 1)
                dve.wait_ge(summed, 1)
                for n, r in enumerate(ROWS):
                    dve.wait_ge(squared, n + 1)
                    dve.tensor_reduce(hq[0:r, n, :], tmp[0:r, n % 2, :].rearrange("p (h v) -> p h v", v=MV), AX, ALU.add
                                      ).then_inc(summed, 1)
                dve.wait_ge(summed, NT + 1)
                dve.tensor_scalar(hq[:], hq[:], 1.0 / MV, EPS, ALU.mult, ALU.add).then_inc(meaned, 1)
                dve.wait_ge(rooted, 1)
                for n, r in enumerate(ROWS):
                    row = rows[0:r, n, :].rearrange("p (h v) -> p h v", v=MV)
                    ch.step(dve.tensor_tensor(row, row, hr[0:r, n, :].unsqueeze(2).broadcast_to([r, MH, MV]), ALU.mult))
                ch.wait()
                for n, r in enumerate(ROWS):
                    ch.step(dve.tensor_tensor(rows[0:r, n, :], rows[0:r, n, :], og[0:r, n, :], ALU.mult))
                ch.wait()

            phases.append(dict(act=act_, pool=pool_, dve=dve_))
            hs.close()

        def finish():
            norm("last_norm", None)
            fin = ExitStack()
            gl = sb("gl", [P, D], where=fin)
            gl_in, gl_done, y_out = sem("gl_in"), sem("gl_done"), sem("y_final")

            def sp_(sp):
                sp.dma_start(gl[:], i["norm_final"].rearrange("(a d) -> a d", a=1).broadcast_to([P, D])).then_inc(gl_in, 16)
                sp.wait_ge(gl_done, NT)
                sp.dma_start(o["y_prompt"].rearrange("a (n p) d -> p (a n) d", p=P), rows[:, 0:NT - 1, :]).then_inc(y_out, 16)
                sp.dma_start(o["y_sample"].rearrange("b s d -> (b s) d"), rows[0:SAMP, NT - 1, :]).then_inc(y_out, 16)
                sp.wait_ge(y_out, 32)

            def dve_(dve):
                dve.wait_ge(gl_in, 16)
                for n, r in enumerate(ROWS):
                    dve.tensor_tensor(rows[0:r, n, :], rows[0:r, n, :], gl[0:r, :], ALU.mult).then_inc(gl_done, 1)

            phases.append(dict(sp=sp_, dve=dve_))
            fin.close()

        fox()
        moe(0)
        mlstm()
        moe(1)
        finish()

        together, cleared = lasting("together"), lasting("cleared")
        taken.extend([] for _ in range(len(phases) - len(taken)))
        block = ctx.enter_context(nc.Block())

        def run(eng, who):
            for n, phase in enumerate(phases):
                if who == "pool" and n:
                    for s in sets[(n - 1) % 2][0:len(taken[n - 1])]:
                        eng.sem_clear(s)
                if who in phase:
                    phase[who](eng)
                if who == "pool":
                    eng.wait_ge(together, 4 * (n + 1))
                    eng.drain().then_inc(cleared, 1)
                else:
                    eng.drain().then_inc(together, 1)
                    eng.wait_ge(cleared, n + 1)
                    alone(eng)

        @block.sync
        def _(sp):
            run(sp, "sp")

        @block.scalar
        def _(act):
            run(act, "act")

        @block.vector
        def _(dve):
            run(dve, "dve")

        @block.gpsimd
        def _(pool):
            run(pool, "pool")

        @block.tensor
        def _(pe):
            run(pe, "pe")


OUTS = [("y_prompt", (1, PROMPT, D)), ("y_sample", (SB, SS, D)),
        ("k_prompt", (1, 1, PROMPT, FH, FD)), ("v_prompt", (1, 1, PROMPT, FH, FD)), ("logf_prompt", (1, 1, PROMPT, FH)),
        ("k_sample", (1, SB, SS, FH, FD)), ("v_sample", (1, SB, SS, FH, FD)), ("logf_sample", (1, SB, SS, FH)),
        ("C_prompt", (1, 1, MH, MK, MV)), ("n_prompt", (1, 1, MH, MK)), ("m_prompt", (1, 1, MH)),
        ("C_sample", (1, SB, MH, MK, MV)), ("n_sample", (1, SB, MH, MK)), ("m_sample", (1, SB, MH))]


def kernel(**inputs):
    import concourse.bacc as _bacc
    from concourse.bass_utils import run_bass_kernel_spmd as _run

    nc = _bacc.Bacc("TRN2", target_bir_lowering=False, num_devices=1)
    arrays, ins, outs = {}, {}, {}
    for name, a in dict(inputs, consts=constants()).items():
        a = np.ascontiguousarray(a)
        arrays["in_" + name] = a
        ins[name] = nc.dram_tensor("in_" + name, a.shape, mybir.dt.from_np(a.dtype), kind="ExternalInput").ap()
    for name, shape in OUTS:
        outs[name] = nc.dram_tensor("out_" + name, shape, F32, kind="ExternalOutput").ap()
    trunk(nc, ins, outs)
    r = _run(nc, [arrays], core_ids=[0])
    return tuple(r.results[0]["out_" + name] for name, _ in OUTS)
```
